# Optimizing a Trainium2 kernel written in Bass

```python
import math
import jax, jax.numpy as jnp
from jax import lax
import numpy as np

"""One inference step (DEPTH layers) of a hybrid decoder trunk serving a prompt group and a sample group with shared weights.

Layer: x += W_o( sigmoid(g_A) * mLSTM_branch(h) + sigmoid(g_B) * shortconv_branch(h) ),  h = RMSNorm(x)
       x += PEER(RMSNorm(x));   final RMSNorm.
All q/k/v/gates/conv inputs/merge gates come from ONE combined input projection w_in.

Inputs:
  x_prompt (BATCH, SEQ, D_MODEL), x_sample (DEC_BATCH, DEC_SEQ, D_MODEL)
  state_mlstm_C (DEPTH, DEC_BATCH, N_HEADS_A, HEAD_DIM, HEAD_DIM)   matrix memory [value, key]
  state_mlstm_n (DEPTH, DEC_BATCH, N_HEADS_A, HEAD_DIM)             normaliser vector
  state_mlstm_m (DEPTH, DEC_BATCH, N_HEADS_A)                       running-max stabiliser
  state_conv    (DEPTH, DEC_BATCH, CONV_WIDTH-1, D_B)               last gated conv-input rows
  then the weights.
Output tuple:
  (y_prompt (BATCH,SEQ,D_MODEL), y_sample (DEC_BATCH,DEC_SEQ,D_MODEL),
   C_prompt (DEPTH,BATCH,H,DH,DH), n_prompt (DEPTH,BATCH,H,DH), m_prompt (DEPTH,BATCH,H), conv_prompt (DEPTH,BATCH,CONV_WIDTH-1,D_B),
   C_sample (DEPTH,DEC_BATCH,H,DH,DH), n_sample (DEPTH,DEC_BATCH,H,DH), m_sample (DEPTH,DEC_BATCH,H), conv_sample (DEPTH,DEC_BATCH,CONV_WIDTH-1,D_B))
"""

D_MODEL = 1024
BATCH = 1
SEQ = 512
DEPTH = 1
DEC_BATCH = 8
DEC_SEQ = 4
PAST_LEN = 4096
PAGE_SIZE = 128

N_HEADS_A = 4
D_A = D_MODEL
HEAD_DIM = D_A // N_HEADS_A
CHUNK = 64
D_B = D_MODEL
CONV_WIDTH = 3
N_KEYS = 128
N_EXPERTS = N_KEYS * N_KEYS
N_RHEADS = 8
D_KEY = 256
D_HALF = D_KEY // 2
TOPK = 16
TOKEN_BLOCK = 128
EPS = 1e-6
IN_COLS = 4 * D_A + 2 * N_HEADS_A + 3 * D_B + 2 * D_MODEL

kernel_name = "hybrid_mlstm_shortconv_peer_step"

def _split_points():
    sizes = (D_A, D_A, D_A, D_A, N_HEADS_A, N_HEADS_A, D_B, D_B, D_B, D_MODEL, D_MODEL)
    return tuple(np.cumsum(sizes)[:-1].tolist())

def rmsnorm(x, g):
    x32 = x.astype(jnp.float32)
    y = x32 * lax.rsqrt(jnp.mean(x32 * x32, axis=-1, keepdims=True) + EPS)
    return (y * g.astype(jnp.float32)).astype(x.dtype)

def mlstm_chunkwise(q, k, v, i_pre, logf, c0, n0, m0):
    b, s, h, d = q.shape
    L = math.gcd(s, CHUNK)
    nc = s // L

    def chunks_vec(t):
        return t.astype(jnp.float32).reshape(b, nc, L, h, d).transpose(1, 0, 3, 2, 4)

    def chunks_gate(t):
        return t.reshape(b, nc, L, h).transpose(1, 0, 3, 2)

    causal = jnp.tril(jnp.ones((L, L), dtype=bool))

    def step(carry, xs):
        c, n, m = carry
        qc, kc, vc, ic, fc = xs
        bcum = jnp.cumsum(fc, axis=-1)
        dmat = bcum[..., :, None] - bcum[..., None, :] + ic[..., None, :]
        dmat = jnp.where(causal, dmat, -jnp.inf)
        inter = bcum + m[..., None]
        m_row = jnp.maximum(inter, jnp.max(dmat, axis=-1))
        w = jnp.exp(dmat - m_row[..., None])
        a = jnp.exp(inter - m_row)
        sw = jnp.einsum('bhtd,bhsd->bhts', qc, kc) * w
        num = a[..., None] * jnp.einsum('bhvk,bhtk->bhtv', c, qc) + jnp.einsum('bhts,bhsv->bhtv', sw, vc)
        den = a * jnp.einsum('bhk,bhtk->bht', n, qc) + jnp.sum(sw, axis=-1)
        hout = num / jnp.maximum(jnp.abs(den), jnp.exp(-m_row))[..., None]
        m_new = m_row[..., -1]
        decay = jnp.exp(bcum[..., -1:] - bcum + ic - m_new[..., None])
        a_end = jnp.exp(bcum[..., -1] + m - m_new)
        c_new = a_end[..., None, None] * c + jnp.einsum('bhs,bhsv,bhsk->bhvk', decay, vc, kc)
        n_new = a_end[..., None] * n + jnp.einsum('bhs,bhsk->bhk', decay, kc)
        return (c_new, n_new, m_new), hout

    carry0 = (c0.astype(jnp.float32), n0.astype(jnp.float32), m0.astype(jnp.float32))
    xs = (chunks_vec(q), chunks_vec(k), chunks_vec(v), chunks_gate(i_pre), chunks_gate(logf))
    (c1, n1, m1), hs = lax.scan(step, carry0, xs)
    hs = hs.transpose(1, 0, 3, 2, 4).reshape(b, s, h, d)
    return hs, c1, n1, m1

def short_conv(u, buf, w):
    s = u.shape[1]
    ext = jnp.concatenate([buf.astype(u.dtype), u], axis=1)
    y = ext[:, 0:s] * w[0]
    for j in range(1, CONV_WIDTH):
        y = y + ext[:, j:j + s] * w[j]
    return y, ext[:, s:]

def hybrid_mixer(h, c0, n0, m0, buf0, w_in, b_if, head_norm, w_out_a, w_out_b, conv_w, w_o):
    bsz, s, _ = h.shape
    proj = jnp.einsum('bsd,dc->bsc', h, w_in)
    q, k, v, o, ig, fg, cb, cc, cx, ga, gb = jnp.split(proj, _split_points(), axis=-1)

    def heads(t):
        return t.reshape(bsz, s, N_HEADS_A, HEAD_DIM)

    i_pre = (ig + b_if[:N_HEADS_A]).astype(jnp.float32)
    logf = jax.nn.log_sigmoid((fg + b_if[N_HEADS_A:]).astype(jnp.float32))
    hcell, c1, n1, m1 = mlstm_chunkwise(heads(q), heads(k) * (HEAD_DIM ** -0.5), heads(v), i_pre, logf, c0, n0, m0)
    hn = hcell * lax.rsqrt(jnp.mean(hcell * hcell, axis=-1, keepdims=True) + EPS) * head_norm.astype(jnp.float32)
    ha = (jax.nn.sigmoid(heads(o).astype(jnp.float32)) * hn).astype(h.dtype).reshape(bsz, s, D_A)
    ya = jnp.einsum('bsc,cd->bsd', ha, w_out_a)

    conv_y, buf1 = short_conv(cc * cx, buf0, conv_w)
    yb = jnp.einsum('bsc,cd->bsd', cb * conv_y, w_out_b)

    merged = jax.nn.sigmoid(ga) * ya + jax.nn.sigmoid(gb) * yb
    out = jnp.einsum('bsd,de->bse', merged, w_o)
    return out, c1, n1, m1, buf1

def peer(h, w_query, keys1, keys2, expert_u, expert_v):
    shp = h.shape
    t = h.reshape(-1, D_MODEL)
    n_tok = t.shape[0]
    pad = (-n_tok) % TOKEN_BLOCK
    t = jnp.pad(t, ((0, pad), (0, 0)))
    blocks = t.reshape(-1, TOKEN_BLOCK, D_MODEL)

    def block_fn(xb):
        qb = jnp.einsum('td,dc->tc', xb, w_query).reshape(TOKEN_BLOCK, N_RHEADS, 2, D_HALF)
        s1 = jnp.einsum('thd,hkd->thk', qb[:, :, 0], keys1).astype(jnp.float32)
        s2 = jnp.einsum('thd,hkd->thk', qb[:, :, 1], keys2).astype(jnp.float32)
        v1, i1 = lax.top_k(s1, TOPK)
        v2, i2 = lax.top_k(s2, TOPK)
        cand = (v1[..., :, None] + v2[..., None, :]).reshape(TOKEN_BLOCK, N_RHEADS, TOPK * TOPK)
        cand_idx = (i1[..., :, None] * N_KEYS + i2[..., None, :]).reshape(TOKEN_BLOCK, N_RHEADS, TOPK * TOPK)
        best, pos = lax.top_k(cand, TOPK)
        idx = jnp.take_along_axis(cand_idx, pos, axis=-1)
        gate = jax.nn.softmax(best, axis=-1)
        u = expert_u[idx]
        act = jax.nn.gelu(jnp.einsum('thkd,td->thk', u, xb).astype(jnp.float32), approximate=False)
        vv = expert_v[idx]
        return jnp.einsum('thk,thkd->td', (gate * act).astype(xb.dtype), vv)

    out = lax.map(block_fn, blocks).reshape(-1, D_MODEL)[:n_tok]
    return out.reshape(shp)

def setup_inputs(seed: int = 0) -> dict:
    key = jax.random.key(seed)
    ks = jax.random.split(key, 24)
    f32 = jnp.float32
    nrm = lambda k, shp, sc: jax.random.normal(k, shp, f32) * sc
    return {
        "x_prompt": nrm(ks[0], (BATCH, SEQ, D_MODEL), 1.0),
        "x_sample": nrm(ks[1], (DEC_BATCH, DEC_SEQ, D_MODEL), 1.0),
        "state_mlstm_C": nrm(ks[2], (DEPTH, DEC_BATCH, N_HEADS_A, HEAD_DIM, HEAD_DIM), HEAD_DIM ** -0.5),
        "state_mlstm_n": nrm(ks[3], (DEPTH, DEC_BATCH, N_HEADS_A, HEAD_DIM), 0.1),
        "state_mlstm_m": nrm(ks[4], (DEPTH, DEC_BATCH, N_HEADS_A), 1.0),
        "state_conv": nrm(ks[5], (DEPTH, DEC_BATCH, CONV_WIDTH - 1, D_B), 1.0),
        "norm_mix": 1.0 + nrm(ks[6], (DEPTH, D_MODEL), 0.05),
        "w_in": nrm(ks[7], (DEPTH, D_MODEL, IN_COLS), D_MODEL ** -0.5),
        "b_if": jnp.concatenate([nrm(ks[8], (DEPTH, N_HEADS_A), 0.1),
                                 3.0 + nrm(ks[9], (DEPTH, N_HEADS_A), 0.5)], axis=-1),
        "head_norm": 1.0 + nrm(ks[10], (DEPTH, N_HEADS_A, HEAD_DIM), 0.05),
        "w_out_a": nrm(ks[11], (DEPTH, D_A, D_MODEL), D_A ** -0.5),
        "w_out_b": nrm(ks[12], (DEPTH, D_B, D_MODEL), D_B ** -0.5),
        "conv_w": nrm(ks[13], (DEPTH, CONV_WIDTH, D_B), CONV_WIDTH ** -0.5),
        "w_o": nrm(ks[14], (DEPTH, D_MODEL, D_MODEL), D_MODEL ** -0.5),
        "norm_ffn": 1.0 + nrm(ks[15], (DEPTH, D_MODEL), 0.05),
        "w_query": nrm(ks[16], (DEPTH, D_MODEL, N_RHEADS * D_KEY), D_MODEL ** -0.5),
        "sub_keys1": nrm(ks[17], (DEPTH, N_RHEADS, N_KEYS, D_HALF), D_HALF ** -0.5),
        "sub_keys2": nrm(ks[18], (DEPTH, N_RHEADS, N_KEYS, D_HALF), D_HALF ** -0.5),
        "expert_u": nrm(ks[19], (DEPTH, N_EXPERTS, D_MODEL), D_MODEL ** -0.5),
        "expert_v": nrm(ks[20], (DEPTH, N_EXPERTS, D_MODEL), N_RHEADS ** -0.5),
        "norm_final": 1.0 + nrm(ks[21], (D_MODEL,), 0.05),
    }

def reference(x_prompt, x_sample, state_mlstm_C, state_mlstm_n, state_mlstm_m, state_conv,
              norm_mix, w_in, b_if, head_norm, w_out_a, w_out_b, conv_w, w_o,
              norm_ffn, w_query, sub_keys1, sub_keys2, expert_u, expert_v, norm_final):
    xp, xs = x_prompt, x_sample
    cp_l, np_l, mp_l, bp_l = [], [], [], []
    cs_l, ns_l, ms_l, bs_l = [], [], [], []
    for l in range(DEPTH):
        mix_w = (w_in[l], b_if[l], head_norm[l], w_out_a[l], w_out_b[l], conv_w[l], w_o[l])
        hp = rmsnorm(xp, norm_mix[l])
        yp, cp, np_, mp, bp = hybrid_mixer(
            hp,
            jnp.zeros((BATCH, N_HEADS_A, HEAD_DIM, HEAD_DIM), jnp.float32),
            jnp.zeros((BATCH, N_HEADS_A, HEAD_DIM), jnp.float32),
            jnp.zeros((BATCH, N_HEADS_A), jnp.float32),
            jnp.zeros((BATCH, CONV_WIDTH - 1, D_B), hp.dtype),
            *mix_w)
        xp = xp + yp
        hs = rmsnorm(xs, norm_mix[l])
        ys, cs, ns, ms, bs = hybrid_mixer(hs, state_mlstm_C[l], state_mlstm_n[l], state_mlstm_m[l],
                                          state_conv[l], *mix_w)
        xs = xs + ys
        peer_w = (w_query[l], sub_keys1[l], sub_keys2[l], expert_u[l], expert_v[l])
        xp = xp + peer(rmsnorm(xp, norm_ffn[l]), *peer_w)
        xs = xs + peer(rmsnorm(xs, norm_ffn[l]), *peer_w)
        cp_l.append(cp.astype(state_mlstm_C.dtype)); np_l.append(np_.astype(state_mlstm_n.dtype))
        mp_l.append(mp.astype(state_mlstm_m.dtype)); bp_l.append(bp.astype(state_conv.dtype))
        cs_l.append(cs.astype(state_mlstm_C.dtype)); ns_l.append(ns.astype(state_mlstm_n.dtype))
        ms_l.append(ms.astype(state_mlstm_m.dtype)); bs_l.append(bs.astype(state_conv.dtype))
    y_prompt = rmsnorm(xp, norm_final)
    y_sample = rmsnorm(xs, norm_final)
    c_p = jnp.stack(cp_l, 0)
    n_p = jnp.stack(np_l, 0)
    m_p = jnp.stack(mp_l, 0)
    conv_p = jnp.stack(bp_l, 0)
    c_s = jnp.stack(cs_l, 0)
    n_s = jnp.stack(ns_l, 0)
    m_s = jnp.stack(ms_l, 0)
    conv_s = jnp.stack(bs_l, 0)
    return (y_prompt, y_sample, c_p, n_p, m_p, conv_p, c_s, n_s, m_s, conv_s)


_drawn_inputs = setup_inputs


def setup_inputs(seed=0):
    import zlib

    import numpy as np

    out = dict(_drawn_inputs(seed))
    spreads = {}
    factors = {}
    for name, (base, spread) in spreads.items():
        noise = np.random.default_rng([zlib.crc32(name.encode()), seed]).standard_normal(out[name].shape)
        drawn = base * np.exp(spread * noise) if base else spread * noise
        out[name] = __import__('jax').numpy.asarray(drawn.astype(out[name].dtype))
    for name, factor in factors.items():
        out[name] = (out[name] * factor).astype(out[name].dtype)
    return out
```

```python
from contextlib import ExitStack

import concourse.bass as bass
from concourse import mybir

F32 = mybir.dt.float32
F32R = mybir.dt.float32r
U32 = mybir.dt.uint32
ALU = mybir.AluOpType
ACT = mybir.ActivationFunctionType
AX_X = mybir.AxisListType.X

P = 128
D = 1024
KT = D // P
SEQ = 512
NSEQ, DSEQ = 8, 4
NSAM = NSEQ * DSEQ
NTOK = SEQ + NSAM
HALF = NTOK // 2
H = 4
DH = D // H
HT = DH // P
SB = SEQ // P
NB = SB + 1
RH = 8
NKEY = 128
TOPK = 16
EPS = 1e-6
NEG = -3.0e38
CHUNKS = NKEY

RING = 4
T_Q, T_K, T_V, T_O, T_GA, T_WA = 0, 8, 16, 24, 32, 40
T_CONV, T_GB, T_WB, T_WO, T_WQ = 48, 72, 80, 88, 96
T_U = T_WQ + 2 * RH
T_VV = T_U + CHUNKS
T_END = T_VV + CHUNKS
AHEAD = RING - 1

ROUTE_TILES = 12
GTOK = 64
UNIT = 4
UNITS_PER_TILE = 2
GROUPS = SEQ // GTOK
TILES_PER_GROUP = GTOK // (UNIT * UNITS_PER_TILE)
LAST_TILES = NSAM // (UNIT * UNITS_PER_TILE)
assert NB * ROUTE_TILES + GROUPS * TILES_PER_GROUP + LAST_TILES == CHUNKS
DGROUPS = CHUNKS // 2

OUTS = {
    "o_y": (P, KT, NTOK), "o_cp": (H, P, HT, DH), "o_np": (P, H * HT), "o_mp": (H, 1),
    "o_convp": (P, KT, 2), "o_cs": (H * NSEQ, P, HT, DH), "o_ns": (P, H * HT, NSEQ),
    "o_ms": (H, NSEQ), "o_convs": (P, KT, NSEQ, 2),
}


def build(nc, x, wtiles, wgate, keysT, c0T, n0T, m0, conv0, vecs, bif, outs):
    ctx = ExitStack()
    with ctx:
        def sem(name):
            return ctx.enter_context(nc.semaphore(name))

        A = KT * NTOK * 4
        base = (nc.sbuf_base + 63) // 64 * 64
        at = {"p": base}

        def put(name, shape, dt=F32, offset=None):
            size = 4
            for s in shape[1:]:
                size *= s
            if offset is None:
                offset = at["p"]
                at["p"] += (size + 31) // 32 * 32
            return nc.alloc_sbuf_tensor_at(name, list(shape), dt, offset=offset)

        w_raw = [put(f"w_raw{r}", [P, KT, P]) for r in range(RING)]
        w_hi = [put(f"w_hi{r}", [P, KT, P], F32R) for r in range(RING)]
        w_lo = [put(f"w_lo{r}", [P, KT, P], F32R) for r in range(RING)]
        ident = put("ident", [P, P])
        ones = put("ones", [P, P])
        causal = put("causal", [P, P])
        iota = put("iota", [P, P])
        iota16 = put("iota16", [P, TOPK])
        sel = put("sel", [H, H, P])
        sam_mask = put("sam_mask", [NSAM, NSEQ, DSEQ])
        seq_mask = put("seq_mask", [NSAM, NSEQ])
        vec = put("vec", [P, 7, KT])
        G_MIX, G_HEAD, G_CONV, G_FFN, G_FINAL = 0, 1, 2, 5, 6
        bias_if = put("bias_if", [P, 1])
        m0_sb = put("m0_sb", [H, NSEQ])
        conv0_sb = put("conv0_sb", [P, KT, NSEQ, 2])
        convp_sb = put("convp_sb", [P, KT, 2])
        convs_sb = put("convs_sb", [P, KT, NSEQ, 2])
        n0_sb = put("n0_sb", [P, H * HT, NSEQ])
        np_sb = put("np_sb", [P, H * HT])
        ns_sb = put("ns_sb", [P, H * HT, NSEQ])
        a_col = put("a_col", [P, NB, H])
        dec_col = put("dec_col", [P, NB, H])
        eps_col = put("eps_col", [P, 1])
        ms_sb = put("ms_sb", [H, NSEQ])
        mp_sb = put("mp_sb", [H, 1])
        R0 = (at["p"] + 63) // 64 * 64
        R = [R0 + k * A for k in range(8)]
        T0 = R0 + 8 * A
        TSIZE = nc.sbuf_usable_end - T0
        L0 = R[5] + 2 * NB * D * 4

        def act_buf(name, k, dt=F32):
            return put(name, [P, KT, 2, HALF], dt, R[k])

        def flat(t):
            return t[:, :, :, :].rearrange("p k a b -> p k (a b)")

        X = act_buf("x_in", 0)
        H_hi, H_lo = act_buf("h_hi", 1, F32R), act_buf("h_lo", 2, F32R)
        Q, K = act_buf("q", 3), act_buf("k", 4)
        VT = act_buf("v_feature", 0)
        HN = act_buf("hn", 0)
        K_tok = put("k_tok", [P, NB, D], F32, R[5])
        V_tok = put("v_tok", [P, NB, D], F32, R[5] + NB * D * 4)
        S_hi, S_lo = act_buf("s_hi", 3, F32R), act_buf("s_lo", 4, F32R)
        SG = act_buf("sg", 5)
        M1 = act_buf("m1", 6)
        M_hi = act_buf("m_hi", 7, F32R)
        M_lo = H_hi
        X_again = act_buf("x_again", 5)
        X2 = act_buf("x2", 0)

        sq = [put(f"sq{n}", [P, 2, HALF], F32, T0 + n * 2176) for n in range(2)]
        rs = put("rs", [P, 2, HALF], F32, T0 + 2 * 2176)
        ht = [put(f"ht{n}", [P, 2, HALF], F32, T0 + (3 + n) * 2176) for n in range(2)]
        wg_raw = put("wg_raw", [P, KT, P], F32, T0 + 5 * 2176)
        wg_hi = put("wg_hi", [P, KT, P], F32R, R[3])
        wg_lo = put("wg_lo", [P, KT, P], F32R, R[3] + 4096)
        GB = R[5]
        grow = [put(f"grow{n}", [64, NTOK], F32, GB + n * 2176) for n in range(12)]
        M_row = put("m_stab", [H, NTOK], F32, T0)
        E_row = put("e_row", [H, NTOK], F32, T0 + 2176)
        W = [put(f"w_sc{n}", [P, SB * SEQ - P * (SB * (SB - 1) // 2)], F32, T0 + 4352 + n * 5120)
             for n in range(2)]
        dV = put("dV", [P, SB, DH], F32, L0)
        C_out = put("c_out", [P, HT, DH], F32, L0 + 4096)
        r_buf = put("r_buf", [P, SEQ], F32, L0 + 6144)
        hsq = put("hsq", [P, SEQ], F32, L0 + 8192)
        assert 8192 + 2048 <= 3 * A - 2 * NB * D * 4
        C0R = 8
        c0_ring = [put(f"c0_ring{n}", [P, HT, DH], F32, R[5] + NB * D * 4 + n * 2048) for n in range(C0R)]
        CNR = 4
        cn_ring = [put(f"cn_ring{n}", [P, HT, DH], F32, R[5] + n * 2048) for n in range(CNR)]
        dVm = put("dVm", [NSAM, NSEQ, DH], F32, R[5] + 8192)
        s_small = T0 + 4352
        Ws = put("ws", [NSAM, H, NSAM], F32, s_small)
        alpha_s = put("alpha_s", [P, H, NSAM], F32, s_small + 512)
        q_al = put("q_al", [P, H * HT, NSAM], F32, s_small + 1024)
        qn = put("qn", [P, H * HT, NSAM], F32, s_small + 2048)
        dm = put("dm", [NSAM, H, NSEQ], F32, s_small + 3072)
        rsam = put("rsam", [P, H, NSAM], F32, s_small + 3200)
        sqs = put("sqs", [P, H * HT, NSAM], F32, s_small + 3712)
        rss = put("rss", [P, H, NSAM], F32, s_small + 4736)
        al_row = put("al_row", [H, NSAM], F32, T0 + 4352 + 10240)
        tmp = [put(f"tmp{n}", [P, 2, HALF], F32, T0 + n * 2176) for n in range(2)]
        cc_t = put("cc_t", [P, 2, HALF], F32, T0 + 2 * 2176)
        u_t = put("u_t", [P, 2, HALF], F32, T0 + 3 * 2176)
        y_t = put("y_t", [P, 2, HALF], F32, T0 + 4 * 2176)
        ext = put("ext", [P, NSEQ, 2 + DSEQ], F32, T0 + 5 * 2176)
        qT = [put(f"qT{n}", [P, 2, HALF], F32, T0 + n * 2176) for n in range(2)]
        keys_sb = put("keys_sb", [P, 2 * RH, NKEY], F32, R[6])
        S_all = put("s_all", [P, NB, 2 * RH, NKEY], F32, R[3])
        o = R[3] + NB * 2 * RH * NKEY * 4
        S_blk = put("s_blk", [P, 2 * RH, NKEY], F32, o)
        cand = put("cand", [P, RH, TOPK, TOPK], F32, o + 8192)
        eq = put("eq", [P, RH, TOPK, TOPK], F32, o + 2 * 8192)
        pr = put("pr", [P, RH, TOPK, TOPK], F32, o + 3 * 8192)
        assert o + 4 * 8192 <= R[3] + 77824
        A_ring = [put(f"a_ring{n}", [P, 2, HALF], F32, T0 + n * 2176) for n in range(4)]
        t1 = T0 + 4 * 2176
        small = {}
        for name, shape, dt in (
            ("val", [P, 2 * RH, TOPK], F32), ("ind", [P, 2 * RH, TOPK], U32), ("indf", [P, 2 * RH, TOPK], F32),
            ("best", [P, RH, TOPK], F32), ("pos", [P, RH, TOPK], U32), ("posw", [P, RH, TOPK], U32),
            ("posf", [P, RH, TOPK], F32), ("e1", [P, RH, TOPK], F32), ("e2", [P, RH, TOPK], F32),
            ("gate", [P, RH, TOPK], F32), ("zsum", [P, RH], F32),
        ):
            small[name] = put(name, shape, dt, t1)
            t1 += shape[1] * (shape[2] if len(shape) > 2 else 1) * 4
        assert t1 <= nc.sbuf_usable_end
        G_st = [put(f"g_st{n}", [P, NKEY, GTOK], F32, R[3] + n * 32768) for n in range(2)]
        oh = R[3] + 65536
        O2 = [put(f"o2_{n}", [P, UNIT, NKEY], F32R, oh + n * 6144) for n in range(2)]
        A1h = [put(f"a1h_{n}", [P, UNIT, NKEY], F32R, oh + n * 6144 + 2048) for n in range(2)]
        A1l = [put(f"a1l_{n}", [P, UNIT, NKEY], F32R, oh + n * 6144 + 4096) for n in range(2)]
        ch = R[3] + 77824
        i1T = put("i1T", [P, NTOK], F32, ch)
        i2T = put("i2T", [P, NTOK], F32, ch + 2176)
        ghT = put("ghT", [P, NTOK], F32R, ch + 2 * 2176)
        glT = put("glT", [P, NTOK], F32, ch + 3 * 2176)
        assert ch + 4 * 2176 <= R[3] + 5 * A
        PA = [put(f"pa{n}", [P, 2, HALF], F32, R[3] + n * 2176) for n in range(4)]
        PG = [put(f"pg{n}", [P, 2, HALF], F32, R[3] + (4 + n) * 2176) for n in range(4)]
        P_hi = [put(f"p_hi{n}", [P, 2, HALF], F32R, R[4] + n * 2176) for n in range(4)]
        P_lo = [put(f"p_lo{n}", [P, 2, HALF], F32R, R[4] + (4 + n) * 2176) for n in range(4)]
        assert TSIZE >= 15 * 1024, TSIZE

        A_dram = nc.dram_tensor("a_scratch", (CHUNKS, P, NTOK), F32).ap()
        G_dram = nc.dram_tensor("g_scratch", (CHUNKS, P, NTOK), F32).ap()

        pair = [ctx.enter_context(nc.psum_tensor(f"pair{n}", [P, 1024], F32)) for n in range(4)]
        pv = [t[:, :].rearrange("p (a b) -> p a b", a=2)[:, :, 0:HALF] for t in pair]

        def bank(n):
            return pair[n // 2][:, 512 * (n % 2):512 * (n % 2) + 512]

        x_in = sem("x_in_loaded")
        consts_in = sem("consts_loaded")
        wg_in = sem("gate_weights_loaded")
        raw_in = [sem(f"raw_loaded{r}") for r in range(RING)]
        hi_made = sem("weights_hi_made")
        lo_made = sem("weights_lo_made")
        tile_done = sem("tile_done")
        out_used = sem("out_used")
        masks_step, masks_made = sem("masks_step"), sem("masks_made")
        sq_made, sq_used, ssq_done, std_made = sem("sq_made"), sem("sq_used"), sem("ssq_done"), sem("std_made")
        ht_made, hh_made, hl_made = sem("ht_made"), sem("hh_made"), sem("hl_made")
        wg_hi_made, wg_lo_made, gate_done = sem("wg_hi_made"), sem("wg_lo_made"), sem("gate_done")
        gate_act = sem("gate_act")
        gate_neg = sem("gate_neg")
        rows_made = sem("rows_made")
        row_args = sem("row_args")
        dve_chain = sem("dve_chain")
        act_chain = sem("act_chain")
        tr_done, tr_k_used, tr_v_used = sem("tr_done"), sem("tr_k_used"), sem("tr_v_used")
        cols_done, cols_used = sem("cols_done"), sem("cols_used")
        s_done, w_arg, w_exp, sw_made = sem("s_done"), sem("w_arg"), sem("w_exp"), sem("sw_made")
        num_done, abs_made, hout_made = sem("num_done"), sem("abs_made"), sem("hout_made")
        hsq_made, hsq_used, hstd_made = sem("hsq_made"), sem("hsq_used"), sem("hstd_made")
        head_done, dv_made, st_done = sem("head_done"), sem("dv_made"), sem("st_done")
        cout_made, cout_stored, n_used = sem("cout_made"), sem("cout_stored"), sem("n_used")
        sam_in = sem("sam_in")
        sb_done, sam_al, sam_arg, sam_exp, sam_sw = (sem("sam_bcast_done"), sem("sam_alpha"), sem("sam_arg"),
                                                     sem("sam_exp"), sem("sam_sw"))
        c0_in = [sem(f"c0_in{n}") for n in range(C0R)]
        upd_done, cn_made = sem("upd_done"), sem("cn_made")
        cn_stored = [sem(f"cn_stored{n}") for n in range(CNR)]
        dvm_made, sam_num = sem("dvm_made"), sem("sam_num")
        sam_abs, sam_hout, sam_sq, sam_rms, sam_std, sam_hn = (sem("sam_abs"), sem("sam_hout"), sem("sam_sq"),
                                                               sem("sam_rms"), sem("sam_std"), sem("sam_hn"))
        t_made, t_hi, t_lo = sem("t_made"), sem("t_hi"), sem("t_lo")
        cc_used = sem("cc_used")
        xa_in = sem("x_again_loaded")
        keys_in = sem("keys_loaded")
        sc_done, sc_used = sem("scores_done"), sem("scores_used")
        blk_made, blk_used = sem("block_copied"), sem("block_used")
        sm_arg, sm_exp, choice_made = sem("softmax_arg"), sem("softmax_exp"), sem("choice_made")
        ct_done, ct_used = sem("choice_turned"), sem("choice_kept")
        onehot_made, g_done, g_used = sem("onehot_made"), sem("gate_units_done"), sem("gate_units_used")
        g_stored = [sem(f"g_stored{n}") for n in range(2)]
        a_stored = [sem(f"a_stored{n}") for n in range(4)]
        ag_in = [sem(f"ag_in{n}") for n in range(4)]
        p_made, p_hi_made, p_lo_made = sem("p_made"), sem("p_hi_made"), sem("p_lo_made")
        down_done, y_used = sem("down_done"), sem("y_used")
        y_made, stored = sem("y_made"), sem("stored")

        block = ctx.enter_context(nc.Block())

        @block.sync
        def _(sp):
            sp.dma_start(flat(X), x).then_inc(x_in, 16)
            for dst, src in ((vec[:, :, :], vecs), (bias_if[:, :], bif), (m0_sb[:, :], m0),
                             (conv0_sb[:, :, :, :], conv0), (n0_sb[:, :, :], n0T)):
                sp.dma_start(dst, src).then_inc(consts_in, 16)
            sp.dma_start(wg_raw[:, :, :], wgate).then_inc(wg_in, 16)

            def load_tile(group, r):
                sp.dma_start(w_raw[r][:, :, :], wtiles[group * RING + r]).then_inc(raw_in[r], 16)

            def load_tiles(first, last):
                with sp.Fori(first, last) as i:
                    for r in range(RING):
                        sp.wait_ge(lo_made, i * RING + (r - RING + 1))
                        load_tile(i, r)

            for r in range(RING):
                load_tile(0, r)
            load_tiles(1, (T_O + RING) // RING)

            sp.wait_ge(st_done, H)
            sp.wait_ge(num_done, H)

            def load_c0(n):
                sp.dma_start(c0_ring[n % C0R][:, :, :], c0T[n]).then_inc(c0_in[n % C0R], 16)

            for n in range(C0R):
                load_c0(n)
            for n in range(H * NSEQ):
                sp.wait_ge(cn_made, n + 1)
                sp.dma_start(outs["o_cs"][n], cn_ring[n % CNR][:, :, :]).then_inc(cn_stored[n % CNR], 16)
                if n + C0R < H * NSEQ:
                    load_c0(n + C0R)
            load_tiles((T_O + RING) // RING, (T_WO + RING) // RING)
            sp.wait_ge(out_used, T_WO + 2)
            sp.dma_start(flat(X_again), x).then_inc(xa_in, 16)
            sp.wait_ge(t_lo, KT * 3)
            sp.dma_start(keys_sb[:, :, :], keysT).then_inc(keys_in, 16)
            load_tiles((T_WO + RING) // RING, (T_VV + RING) // RING)

            for n in range(4):
                sp.wait_ge(a_stored[n], 16 * (CHUNKS // 4))
            for n in range(2):
                sp.wait_ge(g_stored[n], 16 * (GROUPS // 2 + (1 - n)))

            def load_ag(c, s):
                sp.dma_start(PA[s][:, :, :].rearrange("p a b -> p (a b)"), A_dram[c]).then_inc(ag_in[s], 16)
                sp.dma_start(PG[s][:, :, :].rearrange("p a b -> p (a b)"), G_dram[c]).then_inc(ag_in[s], 16)

            for s in range(4):
                load_ag(s, s)
            with sp.Fori(1, CHUNKS // 4) as i:
                for s in range(4):
                    sp.wait_ge(lo_made, i * RING + (T_VV + s - RING + 1))
                    sp.dma_start(w_raw[s][:, :, :], wtiles[i * RING + (T_VV + s)]).then_inc(raw_in[s], 16)
                    sp.wait_ge(p_lo_made, i * 4 + (s - 3))
                    load_ag(i * 4 + s, s)
            n_out = 0
            for name, src, ready, count in (
                ("o_np", np_sb[:, :], n_used, H), ("o_mp", mp_sb[:, :], rows_made, 1),
                ("o_ms", ms_sb[:, :], rows_made, 1), ("o_ns", ns_sb[:, :, :], sam_hn, 1),
                ("o_convp", convp_sb[:, :, :], t_lo, 2 * KT), ("o_convs", convs_sb[:, :, :, :], t_lo, 2 * KT),
            ):
                sp.wait_ge(ready, count)
                sp.dma_start(outs[name], src).then_inc(stored, 16)
                n_out += 1
            for k in range(KT):
                sp.wait_ge(y_made, k + 1)
                sp.dma_start(outs["o_y"][:, k, :], ht[k % 2][:, :, :].rearrange("p a b -> p (a b)")).then_inc(stored, 16)
                n_out += 1
                if k + 2 <= KT:
                    sp.wait_ge(stored, 16 * n_out)
                    sp.sem_inc(hl_made, 1)
            sp.wait_ge(stored, 16 * n_out)
            for n in range(CNR):
                sp.wait_ge(cn_stored[n], 16 * (H * NSEQ // CNR))
            sp.wait_ge(cout_stored, 16 * H)

        @block.gpsimd
        def _(pool):
            pool.memset(ones[:, :], 1.0).then_inc(masks_step, 1)
            pool.memset(ident[:, :], 0.0).then_inc(masks_step, 1)
            pool.memset(causal[:, :], 1.0).then_inc(masks_step, 1)
            pool.memset(sel[:, :, :], 0.0).then_inc(masks_step, 1)
            pool.memset(sam_mask[:, :, :], 1.0).then_inc(masks_step, 1)
            pool.memset(seq_mask[:, :], 1.0).then_inc(masks_step, 1)
            pool.memset(eps_col[:, :], EPS).then_inc(masks_step, 1)
            pool.iota(iota[:, :], [[1, NKEY]], base=0, channel_multiplier=0,
                      allow_small_or_imprecise_dtypes=True).then_inc(masks_step, 1)
            pool.iota(iota16[:, :], [[1, TOPK]], base=0, channel_multiplier=0,
                      allow_small_or_imprecise_dtypes=True).then_inc(masks_step, 1)
            pool.wait_ge(masks_step, 9)
            pool.affine_select(out=ident[:, :], in_=ident[:, :], compare_op=ALU.not_equal, fill=1.0,
                               base=0, pattern=[[-1, P]], channel_multiplier=1).then_inc(masks_step, 1)
            pool.affine_select(out=causal[:, :], in_=causal[:, :], compare_op=ALU.is_ge, fill=0.0,
                               base=0, pattern=[[1, P]], channel_multiplier=-1).then_inc(masks_step, 1)
            pool.affine_select(out=sel[:, :, :], in_=sel[:, :, :], compare_op=ALU.not_equal, fill=1.0,
                               base=0, pattern=[[-1, H], [0, P]], channel_multiplier=1).then_inc(masks_step, 1)
            pool.affine_select(out=sam_mask[:, :, :], in_=sam_mask[:, :, :], compare_op=ALU.is_ge, fill=0.0,
                               base=0, pattern=[[DSEQ, NSEQ], [1, DSEQ]], channel_multiplier=-1).then_inc(masks_step, 1)
            pool.affine_select(out=seq_mask[:, :], in_=seq_mask[:, :], compare_op=ALU.is_ge, fill=0.0,
                               base=0, pattern=[[-DSEQ, NSEQ]], channel_multiplier=1).then_inc(masks_step, 1)
            pool.wait_ge(masks_step, 14)
            pool.affine_select(out=sam_mask[:, :, :], in_=sam_mask[:, :, :], compare_op=ALU.is_ge, fill=0.0,
                               base=0, pattern=[[-DSEQ, NSEQ], [0, DSEQ]], channel_multiplier=1).then_inc(masks_made, 1)
            pool.affine_select(out=seq_mask[:, :], in_=seq_mask[:, :], compare_op=ALU.is_ge, fill=0.0,
                               base=DSEQ - 1, pattern=[[DSEQ, NSEQ]], channel_multiplier=-1).then_inc(masks_made, 1)
            with pool.Fori(0, T_END // RING) as i:
                for r in range(RING):
                    pool.wait_ge(hi_made, i * RING + (r + 1))
                    nc.gpsimd.tensor_tensor(w_lo[r][:, :, :], w_raw[r][:, :, :], w_hi[r][:, :, :].bitcast(F32),
                                            ALU.subtract).then_inc(lo_made, 1)

        @block.tensor
        def _(pe):
            def project(i, t, hi, lo):
                r, out = t % RING, pair[t % 2]
                pe.wait_ge(lo_made, i * RING + (t + 1))
                pe.wait_ge(out_used, i * RING + (t + 1))
                for k in range(KT):
                    for w, xs in ((w_hi, (hi, lo)), (w_lo, (hi,))):
                        for x_part in xs:
                            for a in range(2):
                                mm = nc.tensor.matmul(out[:, 512 * a:512 * a + HALF], w[r][:, k, :],
                                                      x_part[:, k, a, :], start=(k == 0 and w is w_hi and x_part is hi),
                                                      stop=(k == KT - 1 and w is w_lo))
                mm.then_inc(tile_done, 1)

            def project_all(t0, n, hi, lo):
                with pe.Fori(0, n // RING) as i:
                    for r in range(RING):
                        project(i, t0 + r, hi, lo)

            def sum_squares(base):
                for k in range(KT):
                    pe.wait_ge(sq_made, base + k + 1)
                    for a in range(2):
                        mm = nc.tensor.matmul(pair[0][:, 512 * a:512 * a + HALF], ones[:, :], sq[k % 2][:, a, :],
                                              start=(k == 0), stop=(k == KT - 1))
                    mm.then_inc(sq_used, 1)

            pe.wait_ge(masks_made, 2)
            sum_squares(0)
            pe.wait_ge(hl_made, KT)
            pe.wait_ge(wg_lo_made, 1)
            for k in range(KT):
                for w, xs in ((wg_hi, (H_hi, H_lo)), (wg_lo, (H_hi,))):
                    for x_part in xs:
                        for a in range(2):
                            mm = nc.tensor.matmul(pair[1][:, 512 * a:512 * a + HALF], w[:, k, :], x_part[:, k, a, :],
                                                  start=(k == 0 and w is wg_hi and x_part is H_hi),
                                                  stop=(k == KT - 1 and w is wg_lo))
            mm.then_inc(gate_done, 1)
            project_all(T_Q, KT, H_hi, H_lo)
            project_all(T_K, KT, H_hi, H_lo)
            pe.wait_ge(rows_made, 1)
            for b in range(NB):
                n = P if b < SB else NSAM
                for j, row in enumerate((grow[0], grow[1])):
                    mm = nc.tensor.matmul(bank(4)[0:n, (2 * b + j) * H:(2 * b + j + 1) * H], row[0:H, b * P:b * P + n],
                                          ident[0:H, 0:H], start=True, stop=True)
            mm.then_inc(cols_done, 1)
            project_all(T_V, KT, H_hi, H_lo)

            pe.wait_ge(out_used, T_V + KT + 2)
            pe.wait_ge(cols_used, 1)
            units = [(src, b, q) for b in range(NB) for q in range(2) for src in (0, 1)]
            for n, (src, b, q) in enumerate(units):
                if n >= 4:
                    m = (n - 4) // 2 + 1
                    pe.wait_ge(tr_v_used if src else tr_k_used, m)
                rows = P if b < SB else NSAM
                for j in range(4):
                    mm = nc.tensor.transpose(bank(4 + n % 4)[0:rows, j * P:(j + 1) * P],
                                             flat(VT if src else K)[:, 4 * q + j, b * P:b * P + rows], ident[:, :])
                mm.then_inc(tr_done, 1)
            pe.wait_ge(tr_k_used, 2 * NB)
            pe.wait_ge(tr_v_used, 2 * NB)

            off = [0, 512, 1024, 896]
            for h in range(H):
                if h:
                    pe.wait_ge(cout_made, h)
                    pe.wait_ge(n_used, h)
                    pe.wait_ge(hstd_made, h)
                    pe.wait_ge(hout_made, 2 * h)
                nc.tensor.matmul(bank(3), sel[0:H, h, :], M_row[:, 0:SEQ], start=True, stop=True)
                mm = nc.tensor.matmul(bank(4), sel[0:H, h, :], E_row[:, 0:SEQ], start=True, stop=True)
                mm.then_inc(s_done, 1)
                for s in range(SB):
                    n = SEQ - s * P
                    dst = bank(off[s] // 512)[:, off[s] % 512:off[s] % 512 + n]
                    for k in range(HT):
                        mm = nc.tensor.matmul(dst, flat(K)[:, h * HT + k, s * P:s * P + P],
                                              flat(Q)[:, h * HT + k, s * P:SEQ], start=(k == 0), stop=(k == HT - 1))
                mm.then_inc(s_done, 1)
                pe.wait_ge(sw_made, h + 1)
                w_off = 0
                for s in range(SB):
                    n = SEQ - s * P
                    sw = W[h % 2][:, w_off:w_off + n]
                    w_off += n
                    for v in range(HT):
                        nc.tensor.matmul(bank(5 + v)[:, s * P:SEQ], V_tok[:, s, h * DH + v * P:h * DH + (v + 1) * P], sw,
                                         start=(s == 0), stop=(s == SB - 1))
                    mm = nc.tensor.matmul(bank(7)[:, s * P:SEQ], ones[:, :], sw, start=(s == 0), stop=(s == SB - 1))
                mm.then_inc(num_done, 1)
                pe.wait_ge(dv_made, h + 1)
                for k in range(HT):
                    for s in range(SB):
                        kt = K_tok[:, s, h * DH + k * P:h * DH + (k + 1) * P]
                        nc.tensor.matmul(bank(0)[:, k * DH:(k + 1) * DH], kt, dV[:, s, :],
                                         start=(s == 0), stop=(s == SB - 1))
                for k in range(HT):
                    for s in range(SB):
                        kt = K_tok[:, s, h * DH + k * P:h * DH + (k + 1) * P]
                        mm = nc.tensor.matmul(bank(1)[:, k:k + 1], kt, dec_col[:, s, h:h + 1],
                                              start=(s == 0), stop=(s == SB - 1))
                mm.then_inc(st_done, 1)
                for v in range(HT):
                    pe.wait_ge(hsq_made, HT * h + v + 1)
                    mm = nc.tensor.matmul(bank(3), ones[:, :], hsq[:, :], start=(v == 0), stop=(v == HT - 1))
                    mm.then_inc(hsq_used, 1)

            pe.wait_ge(cout_made, H)
            pe.wait_ge(n_used, H)
            pe.wait_ge(hstd_made, H)
            pe.wait_ge(hout_made, 2 * H)
            for h in range(H):
                nc.tensor.matmul(bank(0)[0:NSAM, P + h * NSAM:P + (h + 1) * NSAM], sel[0:H, h, 0:NSAM],
                                 M_row[:, SEQ:NTOK], start=True, stop=True)
                nc.tensor.matmul(bank(1)[:, h * NSAM:(h + 1) * NSAM], sel[0:H, h, :], al_row[:, :], start=True, stop=True)
                nc.tensor.matmul(bank(2)[:, h * NSAM:(h + 1) * NSAM], sel[0:H, h, :], E_row[:, SEQ:NTOK],
                                 start=True, stop=True)
            for h in range(H):
                for k in range(HT):
                    mm = nc.tensor.matmul(bank(0)[0:NSAM, h * NSAM:(h + 1) * NSAM], flat(K)[:, h * HT + k, SEQ:NTOK],
                                          flat(Q)[:, h * HT + k, SEQ:NTOK], start=(k == 0), stop=(k == HT - 1))
            mm.then_inc(sb_done, 1)
            pe.wait_ge(sam_sw, 1)
            for h in range(H):
                nc.tensor.matmul(bank(4)[:, h * NSAM:(h + 1) * NSAM], ones[0:NSAM, :], Ws[:, h, :], start=True, stop=False)
                for k in range(HT):
                    nc.tensor.matmul(bank(4)[:, h * NSAM:(h + 1) * NSAM], ones[:, :], qn[:, h * HT + k, :],
                                     start=False, stop=(k == HT - 1))
            for h in range(H):
                for k in range(HT):
                    mm = nc.tensor.matmul(bank(4)[:, P + (h * HT + k) * NSEQ:P + (h * HT + k + 1) * NSEQ],
                                          K_tok[0:NSAM, SB, h * DH + k * P:h * DH + (k + 1) * P], dm[:, h, :],
                                          start=True, stop=True)
            for h in range(H):
                for v in range(HT):
                    nc.tensor.matmul(bank(5)[:, (h * HT + v) * NSAM:(h * HT + v + 1) * NSAM],
                                     V_tok[0:NSAM, SB, h * DH + v * P:h * DH + (v + 1) * P], Ws[:, h, :],
                                     start=(h == 0 and v == 0), stop=False, skip_group_check=True)
            for h in range(H):
                pe.wait_ge(dvm_made, h + 1)
                for b in range(NSEQ):
                    n = h * NSEQ + b
                    pe.wait_ge(c0_in[n % C0R], 16 * (n // C0R + 1))
                    for v in range(HT):
                        c = (h * HT + v) * NSAM + b * DSEQ
                        for k in range(HT):
                            mm = nc.tensor.matmul(bank(5)[:, c:c + DSEQ], c0_ring[n % C0R][:, k, v * P:(v + 1) * P],
                                                  q_al[:, h * HT + k, b * DSEQ:(b + 1) * DSEQ],
                                                  start=False, stop=(k == HT - 1), skip_group_check=True)
                    if n == H * NSEQ - 1:
                        mm.then_inc(sam_num, 1)
                    if n >= 2:
                        pe.wait_ge(cn_made, n - 1)
                    for k in range(HT):
                        mm = nc.tensor.matmul(bank(6 + n % 2)[:, k * DH:(k + 1) * DH],
                                              K_tok[0:NSAM, SB, h * DH + k * P:h * DH + (k + 1) * P], dVm[:, b, :],
                                              start=True, stop=True)
                    mm.then_inc(upd_done, 1)
            pe.wait_ge(sam_sq, 1)
            for h in range(H):
                for v in range(HT):
                    mm = nc.tensor.matmul(bank(3)[:, h * NSAM:(h + 1) * NSAM], ones[:, :], sqs[:, h * HT + v, :],
                                          start=(v == 0), stop=(v == HT - 1))
            mm.then_inc(sam_rms, 1)

            pe.wait_ge(sam_hn, 1)
            project_all(T_O, KT, H_hi, H_lo)
            project_all(T_GA, KT, H_hi, H_lo)
            pe.wait_ge(t_lo, KT)
            project_all(T_WA, KT, S_hi, S_lo)
            project_all(T_CONV, 3 * KT, H_hi, H_lo)
            project_all(T_GB, KT, H_hi, H_lo)
            pe.wait_ge(t_lo, 2 * KT)
            project_all(T_WB, KT, S_hi, S_lo)
            pe.wait_ge(t_lo, 3 * KT)
            project_all(T_WO, KT, M_hi, M_lo)
            pe.wait_ge(out_used, T_WQ + 2)
            sum_squares(KT)

            def scores(i, j):
                out = pair[2 + j % 2]
                pe.wait_ge(out_used, i * RING + (T_WQ + j + 3))
                pe.wait_ge(sc_used, i * RING + (j + 1))
                for b in range(NB):
                    n = P if b < SB else NSAM
                    mm = nc.tensor.matmul(out[0:n, b * P:(b + 1) * P],
                                          qT[j % 2][:, :, :].rearrange("p a b -> p (a b)")[:, b * P:b * P + n],
                                          keys_sb[:, i * RING + j, :], start=True, stop=True)
                mm.then_inc(sc_done, 1)

            pe.sem_inc(sc_done, 2)
            pe.sem_inc(g_done, 2)
            pe.wait_ge(hl_made, 2 * KT)
            pe.wait_ge(keys_in, 16)
            for r in range(RING):
                project(0, T_WQ + r, H_hi, H_lo)
                if r:
                    scores(0, r - 1)
            with pe.Fori(1, 2 * RH // RING) as i:
                for r in range(RING):
                    project(i, T_WQ + r, H_hi, H_lo)
                    scores(i, r - 1)
            scores(0, 2 * RH - 1)

            pe.wait_ge(sc_used, 2 * RH + 2)

            def up_and_turn(b, n):
                for r in range(ROUTE_TILES):
                    project(b * (ROUTE_TILES // RING), T_U + r, H_hi, H_lo)
                pe.wait_ge(choice_made, b + 1)
                if not (isinstance(b, int) and b == 0):
                    pe.wait_ge(ct_used, b)
                for j, src in enumerate((small["e1"], small["e2"], small["gate"])):
                    mm = nc.tensor.transpose(bank(4)[:, j * P:j * P + n],
                                             src[0:n, :, :].rearrange("p h k -> p (h k)"), ident[0:n, 0:n])
                mm.then_inc(ct_done, 1)

            up_and_turn(0, P)
            with pe.Fori(1, SB) as b:
                up_and_turn(b, P)
            up_and_turn(SB, NSAM)
            pe.wait_ge(ct_used, NB)

            def gate_unit(i, per, u):
                pe.wait_ge(onehot_made, i * per + (u + 1))
                pe.wait_ge(g_used, i * per + (u + 1))
                for q in range(UNIT):
                    for part in (A1h, A1l):
                        mm = nc.tensor.matmul(bank(4 + u % 4)[:, q * NKEY:(q + 1) * NKEY], O2[u % 2][:, q, :],
                                              part[u % 2][:, q, :], start=(part is A1h), stop=(part is A1l))
                mm.then_inc(g_done, 1)

            t0 = T_U + NB * ROUTE_TILES
            with pe.Fori(0, (CHUNKS - NB * ROUTE_TILES) // RING) as i:
                for r in range(RING):
                    project(i, t0 + r, H_hi, H_lo)
                    for u in range(UNITS_PER_TILE):
                        gate_unit(i, RING * UNITS_PER_TILE, UNITS_PER_TILE * r + u)

            def down(i, g):
                pe.wait_ge(lo_made, i * RING + (T_VV + 2 * g + 2))
                pe.wait_ge(p_lo_made, i * RING + (2 * g + 2))
                for d in range(KT):
                    pe.wait_ge(y_used, i * 2 * KT + (KT * g + d + KT - 1))
                    out = pair[d % 2]
                    for c in range(2):
                        r = (2 * g + c) % RING
                        for w, xs in ((w_hi, (P_hi, P_lo)), (w_lo, (P_hi,))):
                            for x_part in xs:
                                for a in range(2):
                                    mm = nc.tensor.matmul(out[:, 512 * a:512 * a + HALF], w[r][:, d, :],
                                                          x_part[r][:, a, :],
                                                          start=(c == 0 and w is w_hi and x_part is P_hi),
                                                          stop=(c == 1 and w is w_lo))
                    mm.then_inc(down_done, 1)

            pe.wait_ge(out_used, T_VV + 2)
            with pe.Fori(0, DGROUPS // 2) as i:
                for g in range(2):
                    down(i, g)
            pe.wait_ge(y_used, KT * (DGROUPS + 1))
            sum_squares(2 * KT)

        @block.scalar
        def _(act):
            links = [0]

            def link(ins):
                links[0] += 1
                ins.then_inc(act_chain, 1)
                act.wait_ge(act_chain, links[0])

            def weights_hi(i, t):
                r = t % RING
                act.wait_ge(raw_in[r], i * 16 + 16 * (t // RING + 1))
                if t >= RING or not isinstance(i, int):
                    act.wait_ge(tile_done, i * RING + (t - RING + 1))
                nc.scalar.activation(w_hi[r][:, :, :], w_raw[r][:, :, :], ACT.Copy).then_inc(hi_made, 1)

            def tile_phase(t0, n, step):
                with act.Fori(0, n // RING) as i:
                    for r in range(RING):
                        weights_hi(i, t0 + r + AHEAD)
                        step(i, t0, r)

            def wait_tile(i, t):
                act.wait_ge(tile_done, i * RING + (t + 1))
                act.wait_ge(out_used, i * RING + (t + 2))

            def squares(src, base, ready=None):
                for k in range(KT):
                    if ready is not None:
                        act.wait_ge(*ready(k))
                    if base + k >= 2:
                        act.wait_ge(sq_used, base + k - 1)
                    nc.scalar.activation(sq[k % 2][:, :, :], src[:, k, :, :], ACT.Square).then_inc(sq_made, 1)

            def std(base):
                act.wait_ge(sq_used, base + KT)
                act.wait_ge(masks_made, 2)
                nc.scalar.activation(rs[:, :, :], pv[0], ACT.Sqrt, bias=eps_col[:, 0:1],
                                     scale=1.0 / D).then_inc(std_made, 1)

            def high_parts(base):
                for k in range(KT):
                    act.wait_ge(ht_made, base + k + 1)
                    nc.scalar.activation(H_hi[:, k, :, :], ht[k % 2][:, :, :], ACT.Copy).then_inc(hh_made, 1)

            act.wait_ge(x_in, 16)
            squares(X, 0)
            std(0)
            act.wait_ge(wg_in, 16)
            nc.scalar.activation(wg_hi[:, :, :], wg_raw[:, :, :], ACT.Copy).then_inc(wg_hi_made, 1)
            high_parts(0)
            for t in range(AHEAD):
                weights_hi(0, t)
            act.wait_ge(gate_neg, 1)
            nc.scalar.activation(grow[3][32:32 + H, :], grow[4][32:32 + H, :], ACT.Exp).then_inc(gate_act, 1)
            act.wait_ge(gate_act, 1)
            nc.scalar.activation(grow[5][32:32 + H, :], grow[3][32:32 + H, :], ACT.Ln, bias=1.0).then_inc(gate_act, 1)
            act.wait_ge(row_args, 3)
            nc.scalar.activation(E_row[:, :], grow[8][0:H, :], ACT.Exp, scale=-1.0).then_inc(gate_act, 1)
            nc.scalar.activation(grow[1][0:H, :], grow[7][0:H, :], ACT.Exp).then_inc(gate_act, 1)
            nc.scalar.activation(al_row[:, :], grow[9][0:H, 0:NSAM], ACT.Exp).then_inc(gate_act, 1)

            for t in range(AHEAD, AHEAD + RING):
                weights_hi(0, t)
            with act.Fori(1, 3 * KT // RING) as i:
                for r in range(RING):
                    weights_hi(i, AHEAD + r)
            for n in range(2 * NB):
                b, q = divmod(n, 2)
                rows = P if b < SB else NSAM
                act.wait_ge(tr_done, 2 * n + 1)
                nc.scalar.activation(K_tok[0:rows, b, q * 512:(q + 1) * 512], bank(4 + (2 * n) % 4)[0:rows, :],
                                     ACT.Copy).then_inc(tr_k_used, 1)

            for h in range(H):
                w_off = 0
                for s in range(SB):
                    n = SEQ - s * P
                    act.wait_ge(w_arg, SB * h + s + 1)
                    nc.scalar.activation(W[h % 2][:, w_off:w_off + n], W[h % 2][:, w_off:w_off + n], ACT.Exp,
                                         scale=-1.0).then_inc(w_exp, 1)
                    w_off += n
                act.wait_ge(num_done, h + 1)
                if h:
                    act.wait_ge(hout_made, 2 * h)
                nc.scalar.activation(r_buf[:, :], bank(7), ACT.Abs).then_inc(abs_made, 1)
                act.wait_ge(st_done, h + 1)
                if h:
                    act.wait_ge(cout_stored, 16 * h)
                nc.scalar.activation(C_out[:, :, :], bank(0).rearrange("p (k v) -> p k v", k=HT),
                                     ACT.Copy).then_inc(cout_made, 1)
                act.wait_ge(cout_made, h + 1)
                act.dma_start(outs["o_cp"][h], C_out[:, :, :]).then_inc(cout_stored, 16)
                for v in range(HT):
                    act.wait_ge(hout_made, HT * h + v + 1)
                    if v:
                        act.wait_ge(hsq_used, HT * h + v)
                    elif h:
                        act.wait_ge(head_done, h)
                    nc.scalar.activation(hsq[:, :], flat(HN)[:, h * HT + v, 0:SEQ], ACT.Square).then_inc(hsq_made, 1)
                act.wait_ge(hsq_used, HT * (h + 1))
                nc.scalar.activation(hsq[:, :], bank(3), ACT.Sqrt, bias=eps_col[:, 0:1],
                                     scale=1.0 / DH).then_inc(hstd_made, 1)

            act.wait_ge(cout_stored, 16 * H)
            act.wait_ge(sb_done, 1)
            nc.scalar.activation(alpha_s[:, :, :], bank(1)[:, 0:P].rearrange("p (h t) -> p h t", h=H),
                                 ACT.Copy).then_inc(sam_al, 1)
            act.wait_ge(sam_arg, 1)
            nc.scalar.activation(Ws[:, :, :], Ws[:, :, :], ACT.Exp, scale=-1.0).then_inc(sam_exp, 1)
            act.wait_ge(sam_num, 1)
            nc.scalar.activation(rsam[:, :, :], bank(4)[:, 0:P].rearrange("p (h t) -> p h t", h=H),
                                 ACT.Abs).then_inc(sam_abs, 1)
            act.wait_ge(sam_hout, 1)
            nc.scalar.activation(sqs[:, :, :], flat(HN)[:, :, SEQ:NTOK], ACT.Square).then_inc(sam_sq, 1)
            act.wait_ge(sam_rms, 1)
            nc.scalar.activation(rss[:, :, :], bank(3)[:, 0:P].rearrange("p (h t) -> p h t", h=H), ACT.Sqrt,
                                 bias=eps_col[:, 0:1], scale=1.0 / DH).then_inc(sam_std, 1)

            def step_o(i, t0, r):
                wait_tile(i, t0 + r)
                nc.scalar.activation(SG[:, i * RING + r, :, :], pv[r % 2], ACT.Sigmoid).then_inc(out_used, 1)
                act.wait_ge(t_made, i * RING + (r + 1))
                nc.scalar.activation(S_hi[:, i * RING + r, :, :], tmp[r % 2][:, :, :], ACT.Copy).then_inc(t_hi, 1)

            tile_phase(T_O, KT, step_o)

            def step_sigmoid(i, t0, r):
                wait_tile(i, t0 + r)
                nc.scalar.activation(SG[:, i * RING + r, :, :], pv[r % 2], ACT.Sigmoid).then_inc(out_used, 1)

            act.wait_ge(t_made, KT)
            tile_phase(T_GA, KT, step_sigmoid)
            tile_phase(T_WA, KT, lambda i, t0, r: None)

            with act.Fori(0, 2) as i:
                for m in range(4):
                    for q in range(3):
                        t = 3 * m + q
                        weights_hi(3 * i, T_CONV + t + AHEAD)
                        if q == 0:
                            wait_tile(3 * i, T_CONV + t)
                            act.wait_ge(cc_used, i * 4 + (m + 1))
                            nc.scalar.activation(cc_t[:, :, :], pv[t % 2], ACT.Copy).then_inc(out_used, 1)
                        if q == 2:
                            act.wait_ge(t_made, i * 4 + (KT + m + 1))
                            nc.scalar.activation(S_hi[:, i * 4 + m, :, :], tmp[m % 2][:, :, :],
                                                 ACT.Copy).then_inc(t_hi, 1)
            act.wait_ge(out_used, T_CONV + 2)
            tile_phase(T_GB, KT, step_sigmoid)

            def step_merge(i, t0, r):
                act.wait_ge(t_made, i * RING + (2 * KT + r + 1))
                nc.scalar.activation(M_hi[:, i * RING + r, :, :], tmp[r % 2][:, :, :], ACT.Copy).then_inc(t_hi, 1)

            tile_phase(T_WB, KT, step_merge)
            tile_phase(T_WO, KT, lambda i, t0, r: None)
            squares(X2, KT, lambda k: (out_used, T_WO + k + 3))
            std(KT)
            high_parts(KT)

            def step_query(i, t0, r):
                wait_tile(i, t0 + r)
                act.wait_ge(sc_done, i * RING + (r + 1))
                nc.scalar.activation(qT[r % 2][:, :, :], pv[r % 2], ACT.Copy).then_inc(out_used, 1)

            tile_phase(T_WQ, 2 * RH, step_query)

            def expert_act(i, t, c, s):
                weights_hi(i, t + AHEAD)
                wait_tile(i, t)
                if not isinstance(i, int) or t >= T_U + 4 or i > 0:
                    act.wait_ge(a_stored[s], i * 16 + 16 * ((t - T_U) // 4))
                nc.scalar.activation(A_ring[s][:, :, :], pv[t % 2], ACT.Gelu).then_inc(out_used, 1)
                act.wait_ge(out_used, i * RING + (t + 3))
                act.dma_start(A_dram[c], A_ring[s][:, :, :].rearrange("p a b -> p (a b)")).then_inc(a_stored[s], 16)

            def route_block(b, n):
                if not isinstance(b, int) or b > 0:
                    act.wait_ge(blk_used, b)
                nc.scalar.activation(S_blk[0:n, :, :], S_all[0:n, b, :, :], ACT.Copy).then_inc(blk_made, 1)
                for r in range(ROUTE_TILES):
                    if r == ROUTE_TILES - 2:
                        act.wait_ge(sm_arg, b + 1)
                        nc.scalar.activation(small["gate"][0:n, :, :], small["gate"][0:n, :, :],
                                             ACT.Exp).then_inc(sm_exp, 1)
                    expert_act(b * (ROUTE_TILES // RING), T_U + r, b * ROUTE_TILES + r, r % 4)

            act.wait_ge(sc_used, 2 * RH + 2)
            route_block(0, P)
            with act.Fori(1, SB) as b:
                route_block(b, P)
            route_block(SB, NSAM)

            def keep_unit(i, per, u, st, col):
                act.wait_ge(g_done, i * per + (u + 3))
                nc.scalar.activation(st[:, :, col:col + UNIT],
                                     bank(4 + u % 4).rearrange("p (q k) -> p k q", q=UNIT),
                                     ACT.Copy).then_inc(g_used, 1)

            act.sem_inc(g_used, 4)
            t0 = T_U + NB * ROUTE_TILES
            upg = TILES_PER_GROUP * UNITS_PER_TILE

            def gate_groups(i):
                for n in range(2):
                    if not isinstance(i, int):
                        act.wait_ge(g_stored[n], i * 16)
                    for r in range(TILES_PER_GROUP):
                        t = t0 + n * TILES_PER_GROUP + r
                        expert_act(i * (2 * TILES_PER_GROUP // RING), t,
                                   i * (2 * TILES_PER_GROUP) + (t - T_U), (t - T_U) % 4)
                        for u in range(UNITS_PER_TILE):
                            keep_unit(i, 2 * upg, n * upg + UNITS_PER_TILE * r + u, G_st[n],
                                      UNIT * (UNITS_PER_TILE * r + u))
                    act.wait_ge(g_used, i * (2 * upg) + ((n + 1) * upg + 4))
                    act.dma_start(G_dram[:, :, bass.ds(i * (2 * GTOK) + n * GTOK, GTOK)].rearrange("c p t -> p c t"),
                                  G_st[n][:, :, :]).then_inc(g_stored[n], 16)

            gate_groups(0)
            with act.Fori(1, GROUPS // 2) as i:
                gate_groups(i)
            act.wait_ge(g_stored[0], 16 * (GROUPS // 2))
            for r in range(LAST_TILES):
                t = T_U + CHUNKS - LAST_TILES + r
                expert_act(0, t, t - T_U, (t - T_U) % 4)
                for u in range(UNITS_PER_TILE):
                    keep_unit(0, 0, GROUPS * upg + UNITS_PER_TILE * r + u, G_st[0], UNIT * (UNITS_PER_TILE * r + u))
            act.wait_ge(g_used, GROUPS * upg + LAST_TILES * UNITS_PER_TILE + 4)
            act.dma_start(G_dram[:, :, SEQ:NTOK].rearrange("c p t -> p c t"),
                          G_st[0][:, :, 0:NSAM]).then_inc(g_stored[0], 16)

            weights_hi(0, T_VV + AHEAD)

            for c in range(2):
                act.wait_ge(p_made, c + 1)
                nc.scalar.activation(P_hi[c][:, :, :], PA[c][:, :, :], ACT.Copy).then_inc(p_hi_made, 1)

            def down_group(i, g, weights):
                for c in (2 * g + 2, 2 * g + 3):
                    if not isinstance(i, int) or g > 0:
                        act.wait_ge(down_done, i * 2 * KT + KT * g)
                    act.wait_ge(p_made, i * RING + (c + 1))
                    nc.scalar.activation(P_hi[c % 4][:, :, :], PA[c % 4][:, :, :], ACT.Copy).then_inc(p_hi_made, 1)
                if weights:
                    for c in (2 * g, 2 * g + 1):
                        act.wait_ge(raw_in[c % 4], i * 16 + 16 * ((T_VV + RING + c) // RING + 1))
                        act.wait_ge(down_done, i * 2 * KT + KT * (g + 1))
                        nc.scalar.activation(w_hi[c % 4][:, :, :], w_raw[c % 4][:, :, :], ACT.Copy).then_inc(hi_made, 1)

            for g in range(2):
                down_group(0, g, True)
            with act.Fori(1, DGROUPS // 2 - 1) as i:
                for g in range(2):
                    down_group(i, g, True)
            down_group(0, DGROUPS - 2, False)
            act.wait_ge(y_used, KT * (DGROUPS + 1))
            squares(X2, 2 * KT)
            std(2 * KT)

        @block.vector
        def _(dve):
            links = [0]

            def link(ins):
                links[0] += 1
                ins.then_inc(dve_chain, 1)
                dve.wait_ge(dve_chain, links[0])

            def normalise(src, gain, base, split):
                dve.wait_ge(std_made, base // KT + 1)
                nc.vector.reciprocal(rs[:, :, :], rs[:, :, :]).then_inc(out_used if base == 0 else dve_chain, 1)
                if base == 0:
                    dve.wait_ge(out_used, 1)
                else:
                    links[0] += 1
                    dve.wait_ge(dve_chain, links[0])

                def low(k):
                    dve.wait_ge(hh_made, base + k + 1)
                    nc.vector.tensor_tensor(H_lo[:, k, :, :], ht[k % 2][:, :, :], H_hi[:, k, :, :].bitcast(F32),
                                            ALU.subtract).then_inc(hl_made, 1)

                for k in range(KT):
                    if k >= 2:
                        dve.wait_ge(hl_made, base + k - 1)
                    nc.vector.scalar_tensor_tensor(out=ht[k % 2][:, :, :], in0=src[:, k, :, :],
                                                   scalar=vec[:, gain, k:k + 1], in1=rs[:, :, :], op0=ALU.mult,
                                                   op1=ALU.mult).then_inc(ht_made if split else y_made, 1)
                    if split and k:
                        low(k - 1)
                if split:
                    low(KT - 1)

            dve.wait_ge(consts_in, 16 * 5)
            dve.wait_ge(wg_hi_made, 1)
            nc.vector.tensor_tensor(wg_lo[:, :, :], wg_raw[:, :, :], wg_hi[:, :, :].bitcast(F32),
                                    ALU.subtract).then_inc(wg_lo_made, 1)
            dve.wait_ge(x_in, 16)
            normalise(X, G_MIX, 0, True)

            dve.wait_ge(gate_done, 1)
            F = slice(32, 32 + H)
            HS = slice(0, H)
            gv = [g[:, :].rearrange("p (a b) -> p a b", a=2) for g in grow]
            link(nc.vector.tensor_scalar(gv[2][F], pv[1][F], bias_if[F, :], None, ALU.add))
            nc.vector.scalar_tensor_tensor(out=gv[4][F], in0=gv[2][F], scalar=-1.0, in1=gv[2][F], op0=ALU.mult,
                                           op1=ALU.min).then_inc(gate_neg, 1)
            link(nc.vector.tensor_scalar(gv[6][HS], pv[1][HS], bias_if[HS, :], None, ALU.add))
            link(nc.vector.tensor_scalar(grow[2][F, :], grow[2][F, :], 0.0, None, ALU.min))
            dve.sem_inc(out_used, 1)
            dve.sem_inc(sc_used, 2)
            dve.sem_inc(cc_used, 1)
            dve.sem_inc(y_used, KT)
            dve.wait_ge(gate_act, 2)
            logf, bcum, ones_row = grow[10], grow[11], grow[9]
            link(nc.vector.tensor_tensor(logf[HS, :], grow[2][F, :], grow[5][F, :], ALU.subtract))
            link(nc.vector.memset(ones_row[HS, :], 1.0))
            link(nc.vector.tensor_tensor_scan(bcum[HS, 0:SEQ], ones_row[HS, 0:SEQ], logf[HS, 0:SEQ], 0.0,
                                              ALU.mult, ALU.add))

            def sam(t, j):
                return t[HS, SEQ:NTOK].rearrange("p (b j) -> p b j", j=DSEQ)[:, :, j]

            link(nc.vector.tensor_copy(sam(bcum, 0), sam(logf, 0)))
            for j in range(1, DSEQ):
                link(nc.vector.tensor_tensor(sam(bcum, j), sam(bcum, j - 1), sam(logf, j), ALU.add))
            a_row = grow[0]
            link(nc.vector.tensor_tensor(a_row[HS, :], grow[6][HS, :], bcum[HS, :], ALU.subtract))
            link(nc.vector.tensor_tensor_scan(M_row[:, 0:SEQ], a_row[HS, 0:SEQ], a_row[HS, 0:SEQ], 0.0,
                                              ALU.max, ALU.max))
            link(nc.vector.tensor_tensor(sam(M_row, 0), m0_sb[:, :], sam(a_row, 0), ALU.max))
            for j in range(1, DSEQ):
                link(nc.vector.tensor_tensor(sam(M_row, j), sam(M_row, j - 1), sam(a_row, j), ALU.max))
            link(nc.vector.tensor_tensor(grow[8][HS, :], bcum[HS, :], M_row[:, :], ALU.add))
            nc.vector.tensor_copy(mp_sb[:, :], grow[8][HS, SEQ - 1:SEQ])
            nc.vector.tensor_copy(ms_sb[:, :], sam(grow[8], DSEQ - 1)).then_inc(row_args, 1)
            nc.vector.tensor_scalar(grow[7][HS, 0:SEQ], a_row[HS, 0:SEQ], M_row[:, SEQ - 1:SEQ], None, ALU.subtract)
            seqs = lambda t: t[HS, SEQ:NTOK].rearrange("p (b j) -> p b j", j=DSEQ)
            nc.vector.tensor_tensor(seqs(grow[7]), seqs(a_row),
                                    sam(M_row, DSEQ - 1).unsqueeze(2).broadcast_to([H, NSEQ, DSEQ]),
                                    ALU.subtract).then_inc(row_args, 1)
            nc.vector.tensor_tensor(grow[9][HS, 0:NSAM].rearrange("p (b j) -> p b j", j=DSEQ),
                                    m0_sb[:, :].unsqueeze(2).broadcast_to([H, NSEQ, DSEQ]), seqs(M_row),
                                    ALU.subtract).then_inc(row_args, 1)
            dve.wait_ge(gate_act, 5)
            dve.sem_inc(rows_made, 1)

            def tile_phase(t0, n, step):
                with dve.Fori(0, n // RING) as i:
                    for r in range(RING):
                        dve.wait_ge(tile_done, i * RING + (t0 + r + 1))
                        step(i, r)

            tile_phase(T_Q, KT, lambda i, r: nc.vector.tensor_copy(
                Q[:, i * RING + r, :, :], pv[r % 2]).then_inc(out_used, 1))
            tile_phase(T_K, KT, lambda i, r: nc.vector.tensor_scalar(
                K[:, i * RING + r, :, :], pv[r % 2], float(DH) ** -0.5, None, ALU.mult).then_inc(out_used, 1))
            dve.wait_ge(cols_done, 1)
            for n, (lo_b, hi_b) in ((P, (0, SB)), (NSAM, (SB, NB))):
                cols = bank(4)[0:n, 0:NB * 2 * H].rearrange("p (b j h) -> p b j h", j=2, h=H)
                nc.vector.tensor_copy(a_col[0:n, lo_b:hi_b, :], cols[:, lo_b:hi_b, 0, :])
                ins = nc.vector.tensor_copy(dec_col[0:n, lo_b:hi_b, :], cols[:, lo_b:hi_b, 1, :])
            ins.then_inc(cols_used, 1)
            tile_phase(T_V, KT, lambda i, r: nc.vector.tensor_copy(
                VT[:, i * RING + r, :, :], pv[r % 2]).then_inc(out_used, 1))
            for n in range(2 * NB):
                b, q = divmod(n, 2)
                rows = P if b < SB else NSAM
                dve.wait_ge(tr_done, 2 * n + 2)
                nc.vector.tensor_copy(V_tok[0:rows, b, q * 512:(q + 1) * 512],
                                      bank(4 + (2 * n + 1) % 4)[0:rows, :]).then_inc(tr_v_used, 1)

            dve.wait_ge(cols_used, 1)
            for h in range(H):
                dve.wait_ge(s_done, 2 * h + 1)
                w_off = []
                c = 0
                for s in range(SB):
                    w_off.append(c)
                    n = SEQ - s * P
                    nc.vector.tensor_scalar(W[h % 2][:, c:c + n], bank(3)[:, s * P:SEQ], a_col[:, s, h:h + 1], 0.0,
                                            ALU.subtract, ALU.max).then_inc(w_arg, 1)
                    c += n
                if h:
                    dve.wait_ge(st_done, h)
                nc.vector.tensor_tensor(dV[:, :, :], V_tok[:, 0:SB, h * DH:(h + 1) * DH],
                                        dec_col[:, 0:SB, h:h + 1].broadcast_to([P, SB, DH]), ALU.mult).then_inc(dv_made, 1)
                dve.wait_ge(w_exp, SB * (h + 1))
                for s in range(SB):
                    d = W[h % 2][:, w_off[s]:w_off[s] + P]
                    ins = nc.vector.tensor_tensor(d, d, causal[:, :], ALU.mult)
                link(ins)
                dve.wait_ge(s_done, 2 * h + 2)
                for s, off in enumerate((0, 512, 1024, 896)):
                    n = SEQ - s * P
                    w = W[h % 2][:, w_off[s]:w_off[s] + n]
                    ins = nc.vector.tensor_tensor(w, bank(off // 512)[:, off % 512:off % 512 + n], w, ALU.mult)
                ins.then_inc(sw_made, 1)
                dve.wait_ge(abs_made, h + 1)
                link(nc.vector.tensor_tensor(r_buf[:, :], r_buf[:, :], bank(4), ALU.max))
                link(nc.vector.reciprocal(r_buf[:, :], r_buf[:, :]))
                for v in range(HT):
                    nc.vector.tensor_tensor(flat(HN)[:, h * HT + v, 0:SEQ], bank(5 + v), r_buf[:, :],
                                            ALU.mult).then_inc(hout_made, 1)
                dve.wait_ge(st_done, h + 1)
                nc.vector.tensor_copy(np_sb[:, h * HT:(h + 1) * HT], bank(1)[:, 0:HT]).then_inc(n_used, 1)
                dve.wait_ge(hstd_made, h + 1)
                link(nc.vector.reciprocal(hsq[:, :], hsq[:, :]))
                for v in range(HT):
                    hn = flat(HN)[:, h * HT + v, 0:SEQ]
                    ins = nc.vector.scalar_tensor_tensor(out=hn, in0=hn, scalar=vec[:, G_HEAD, h * HT + v:h * HT + v + 1],
                                                         in1=hsq[:, :], op0=ALU.mult, op1=ALU.mult)
                ins.then_inc(head_done, 1)

            def heads(ap):
                return ap.rearrange("p (h t) -> p h t", h=H)

            dve.wait_ge(sb_done, 1)
            nc.vector.tensor_tensor(dm[:, :, :], dec_col[0:NSAM, SB, :].unsqueeze(2).broadcast_to([NSAM, H, NSEQ]),
                                    seq_mask[:, :].unsqueeze(1).broadcast_to([NSAM, H, NSEQ]), ALU.mult)
            link(nc.vector.tensor_tensor(Ws[:, :, :], heads(bank(0)[0:NSAM, P:2 * P]),
                                         a_col[0:NSAM, SB, :].unsqueeze(2).broadcast_to([NSAM, H, NSAM]), ALU.subtract))
            nc.vector.tensor_scalar(Ws[:, :, :], Ws[:, :, :], 0.0, None, ALU.max).then_inc(sam_arg, 1)
            dve.wait_ge(sam_al, 1)
            link(nc.vector.tensor_tensor(
                q_al[:, :, :].rearrange("p (h k) t -> p h k t", k=HT),
                flat(Q)[:, :, SEQ:NTOK].rearrange("p (h k) t -> p h k t", k=HT),
                alpha_s[:, :, :].unsqueeze(2).broadcast_to([P, H, HT, NSAM]), ALU.mult))
            nc.vector.tensor_tensor(qn[:, :, :].rearrange("p f (b j) -> p f b j", j=DSEQ),
                                    q_al[:, :, :].rearrange("p f (b j) -> p f b j", j=DSEQ),
                                    n0_sb[:, :, :].unsqueeze(3).broadcast_to([P, H * HT, NSEQ, DSEQ]), ALU.mult)
            dve.wait_ge(sam_exp, 1)
            link(nc.vector.tensor_tensor(Ws[:, :, :], Ws[:, :, :], sam_mask[:, :, :].rearrange("p b j -> p (b j)")
                                         .unsqueeze(1).broadcast_to([NSAM, H, NSAM]), ALU.mult))
            nc.vector.tensor_tensor(Ws[:, :, :], heads(bank(0)[0:NSAM, 0:P]), Ws[:, :, :], ALU.mult).then_inc(sam_sw, 1)
            for h in range(H):
                if h:
                    dve.wait_ge(upd_done, NSEQ * h)
                nc.vector.tensor_tensor(
                    dVm[:, :, :], V_tok[0:NSAM, SB, h * DH:(h + 1) * DH].unsqueeze(1).broadcast_to([NSAM, NSEQ, DH]),
                    dm[:, h, :].unsqueeze(2).broadcast_to([NSAM, NSEQ, DH]), ALU.mult).then_inc(dvm_made, 1)
                for b in range(NSEQ):
                    n = h * NSEQ + b
                    dve.wait_ge(upd_done, n + 1)
                    if n >= CNR:
                        dve.wait_ge(cn_stored[n % CNR], 16 * (n // CNR))
                    nc.vector.scalar_tensor_tensor(
                        out=cn_ring[n % CNR][:, :, :].rearrange("p k v -> p (k v)"),
                        in0=c0_ring[n % C0R][:, :, :].rearrange("p k v -> p (k v)"),
                        scalar=alpha_s[:, h, b * DSEQ + DSEQ - 1:b * DSEQ + DSEQ], in1=bank(6 + n % 2), op0=ALU.mult,
                        op1=ALU.add).then_inc(cn_made, 1)
            a_end = alpha_s[:, :, :].rearrange("p h (b j) -> p h b j", j=DSEQ)[:, :, :, DSEQ - 1]
            link(nc.vector.tensor_tensor(ns_sb[:, :, :].rearrange("p (h k) b -> p h k b", k=HT),
                                         n0_sb[:, :, :].rearrange("p (h k) b -> p h k b", k=HT),
                                         a_end.unsqueeze(2).broadcast_to([P, H, HT, NSEQ]), ALU.mult))
            dve.wait_ge(sam_abs, 1)
            nc.vector.tensor_tensor(ns_sb[:, :, :], bank(4)[:, P:P + H * HT * NSEQ].rearrange("p (f b) -> p f b", b=NSEQ),
                                    ns_sb[:, :, :], ALU.add)
            link(nc.vector.tensor_tensor(rsam[:, :, :], rsam[:, :, :], heads(bank(2)[:, 0:P]), ALU.max))
            link(nc.vector.reciprocal(rsam[:, :, :], rsam[:, :, :]))
            hs = flat(HN)[:, :, SEQ:NTOK]
            hs4 = hs.rearrange("p (h k) t -> p h k t", k=HT)
            nc.vector.tensor_tensor(hs4, bank(5)[:, 0:2 * P].rearrange("p (h k t) -> p h k t", h=H, k=HT),
                                    rsam[:, :, :].unsqueeze(2).broadcast_to([P, H, HT, NSAM]),
                                    ALU.mult).then_inc(sam_hout, 1)
            dve.wait_ge(sam_std, 1)
            link(nc.vector.reciprocal(rss[:, :, :], rss[:, :, :]))
            dve.wait_ge(sam_hout, 1)
            link(nc.vector.tensor_tensor(hs4, hs4, rss[:, :, :].unsqueeze(2).broadcast_to([P, H, HT, NSAM]), ALU.mult))
            link(nc.vector.tensor_tensor(hs, hs, vec[:, G_HEAD, :].unsqueeze(2).broadcast_to([P, KT, NSAM]), ALU.mult))
            dve.wait_ge(head_done, H)
            for n in range(CNR):
                dve.wait_ge(cn_stored[n], 16 * (H * NSEQ // CNR))
            dve.sem_inc(sam_hn, 1)

            def low(i, j, n, lo, hi, dst, count):
                dve.wait_ge(t_hi, count)
                nc.vector.tensor_tensor(lo[:, dst, :, :], tmp[n][:, :, :], hi[:, dst, :, :].bitcast(F32),
                                        ALU.subtract).then_inc(t_lo, 1)
                dve.wait_ge(t_lo, count)

            def step_ha(i, r):
                j = i * RING + r
                dve.wait_ge(out_used, i * RING + (T_O + r + 3))
                nc.vector.tensor_tensor(tmp[r % 2][:, :, :], SG[:, j, :, :], HN[:, j, :, :], ALU.mult).then_inc(t_made, 1)
                low(i, j, r % 2, S_lo, S_hi, j, i * RING + (r + 1))

            tile_phase(T_O, KT, step_ha)
            dve.wait_ge(out_used, T_WA + 2)
            tile_phase(T_WA, KT, lambda i, r: nc.vector.tensor_tensor(
                M1[:, i * RING + r, :, :], pv[r % 2], SG[:, i * RING + r, :, :], ALU.mult).then_inc(out_used, 1))

            conv_steps = 9
            conv_base = links[0]
            with dve.Fori(0, 2) as i:
                for m in range(4):
                    j = i * 4 + m
                    k0 = [m * conv_steps]

                    def clink(ins):
                        k0[0] += 1
                        ins.then_inc(dve_chain, 1)
                        dve.wait_ge(dve_chain, i * (4 * conv_steps) + (conv_base + k0[0]))

                    uf = u_t[:, :, :].rearrange("p a b -> p (a b)")
                    yf = y_t[:, :, :].rearrange("p a b -> p (a b)")
                    dve.wait_ge(out_used, i * 12 + (T_CONV + 3 * m + 3))
                    dve.wait_ge(tile_done, i * 12 + (T_CONV + 3 * m + 2))
                    nc.vector.tensor_tensor(u_t[:, :, :], pv[(3 * m + 1) % 2], cc_t[:, :, :], ALU.mult).then_inc(out_used, 1)
                    dve.wait_ge(out_used, i * 12 + (T_CONV + 3 * m + 4))
                    dve.sem_inc(cc_used, 1)
                    wc = [vec[:, G_CONV + q, bass.ds(j, 1)] for q in range(3)]
                    clink(nc.vector.tensor_scalar(y_t[:, :, :], u_t[:, :, :], wc[2], None, ALU.mult))
                    for q, lag in ((1, 1), (0, 2)):
                        clink(nc.vector.scalar_tensor_tensor(out=yf[:, lag:SEQ], in0=uf[:, 0:SEQ - lag], scalar=wc[q],
                                                             in1=yf[:, lag:SEQ], op0=ALU.mult, op1=ALU.add))
                    clink(nc.vector.tensor_copy(ext[:, :, 0:2], conv0_sb[:, j, :, :]))
                    clink(nc.vector.tensor_copy(ext[:, :, 2:2 + DSEQ],
                                                uf[:, SEQ:NTOK].rearrange("p (b j) -> p b j", j=DSEQ)))
                    ys = yf[:, SEQ:NTOK].rearrange("p (b j) -> p b j", j=DSEQ)
                    for q in (1, 0):
                        clink(nc.vector.scalar_tensor_tensor(out=ys, in0=ext[:, :, q:q + DSEQ], scalar=wc[q], in1=ys,
                                                             op0=ALU.mult, op1=ALU.add))
                    clink(nc.vector.tensor_copy(convp_sb[:, j, :], uf[:, SEQ - 2:SEQ]))
                    clink(nc.vector.tensor_copy(convs_sb[:, j, :, :], ext[:, :, DSEQ:DSEQ + 2]))
                    dve.wait_ge(tile_done, i * 12 + (T_CONV + 3 * m + 3))
                    nc.vector.tensor_tensor(tmp[m % 2][:, :, :], pv[(3 * m + 2) % 2], y_t[:, :, :],
                                            ALU.mult).then_inc(t_made, 1)
                    dve.wait_ge(t_made, i * 4 + (KT + m + 1))
                    dve.sem_inc(out_used, 1)
                    low(i, j, m % 2, S_lo, S_hi, j, i * 4 + (KT + m + 1))
            links[0] += 8 * conv_steps

            def step_merge(i, r):
                j = i * RING + r
                nc.vector.tensor_tensor(tmp[r % 2][:, :, :], pv[r % 2], SG[:, j, :, :], ALU.mult).then_inc(out_used, 1)
                dve.wait_ge(out_used, i * RING + (T_WB + r + 3))
                nc.vector.tensor_tensor(tmp[r % 2][:, :, :], tmp[r % 2][:, :, :], M1[:, j, :, :],
                                        ALU.add).then_inc(t_made, 1)
                low(i, j, r % 2, M_lo, M_hi, j, i * RING + (2 * KT + r + 1))

            dve.wait_ge(out_used, T_WB + 2)
            tile_phase(T_WB, KT, step_merge)
            dve.wait_ge(xa_in, 16)
            tile_phase(T_WO, KT, lambda i, r: nc.vector.tensor_tensor(
                X2[:, i * RING + r, :, :], pv[r % 2], X_again[:, i * RING + r, :, :], ALU.add).then_inc(out_used, 1))
            normalise(X2, G_FFN, KT, True)

            with dve.Fori(0, 2 * RH // RING) as i:
                for r in range(RING):
                    dve.wait_ge(sc_done, i * RING + (r + 3))
                    j = i * RING + r
                    nc.vector.tensor_copy(S_all[:, 0:SB, j, :],
                                          pair[2 + r % 2][:, 0:SB * P].rearrange("p (b k) -> p b k", k=NKEY))
                    nc.vector.tensor_copy(S_all[0:NSAM, SB, j, :],
                                          pair[2 + r % 2][0:NSAM, SB * P:NB * P]).then_inc(sc_used, 1)

            def route(b, n):
                val, ind, indf = small["val"], small["ind"], small["indf"]
                best, pos, posw, posf = small["best"], small["pos"], small["posw"], small["posf"]
                e1, e2, gate, zsum = small["e1"], small["e2"], small["gate"], small["zsum"]

                def top16(src, vals, inds, rows):
                    for half in range(2):
                        c = slice(8 * half, 8 * half + 8)
                        for j in range(rows):
                            ins = nc.vector.max(vals[0:n, j, c], src(j))
                        link(ins)
                        for j in range(rows):
                            ins = nc.vector.max_index(inds[0:n, j, c], vals[0:n, j, c], src(j))
                        link(ins)
                        if half == 0:
                            for j in range(rows):
                                ins = nc.vector.match_replace(out=src(j), in_to_replace=vals[0:n, j, c],
                                                              in_values=src(j), imm_value=NEG)
                            link(ins)

                dve.wait_ge(blk_made, b + 1)
                top16(lambda j: S_blk[0:n, j, :], val, ind, 2 * RH)
                dve.sem_inc(blk_used, 1)
                v4 = val[0:n, :, :].rearrange("p (h s) k -> p h s k", s=2)
                full = [n, RH, TOPK, TOPK]
                nc.vector.tensor_copy(indf[0:n, :, :], ind[0:n, :, :])
                link(nc.vector.tensor_tensor(cand[0:n, :, :, :], v4[:, :, 0, :].unsqueeze(3).broadcast_to(full),
                                              v4[:, :, 1, :].unsqueeze(2).broadcast_to(full), ALU.add))
                top16(lambda h: cand[0:n, h, :, :].rearrange("p a b -> p (a b)"), best, pos, RH)
                link(nc.vector.tensor_tensor(gate[0:n, :, :], best[0:n, :, :],
                                              best[0:n, :, 0:1].broadcast_to([n, RH, TOPK]), ALU.subtract))
                dve.sem_inc(sm_arg, 1)
                i4 = indf[0:n, :, :].rearrange("p (h s) k -> p h s k", s=2)
                for s, out in ((0, e1), (1, e2)):
                    if s == 0:
                        link(nc.vector.tensor_scalar(posw[0:n, :, :], pos[0:n, :, :], 4, None, ALU.logical_shift_right))
                    else:
                        link(nc.vector.tensor_scalar(posw[0:n, :, :], pos[0:n, :, :], TOPK - 1, None, ALU.bitwise_and))
                    link(nc.vector.tensor_copy(posf[0:n, :, :], posw[0:n, :, :]))
                    link(nc.vector.tensor_tensor(eq[0:n, :, :, :], posf[0:n, :, :].unsqueeze(3).broadcast_to(full),
                                                  iota16[0:n, :].unsqueeze(1).unsqueeze(1).broadcast_to(full),
                                                  ALU.is_equal))
                    link(nc.vector.tensor_tensor(pr[0:n, :, :, :], eq[0:n, :, :, :],
                                                  i4[:, :, s, :].unsqueeze(2).broadcast_to(full), ALU.mult))
                    link(nc.vector.tensor_reduce(out[0:n, :, :], pr[0:n, :, :, :], AX_X, ALU.add))
                dve.wait_ge(sm_exp, b + 1)
                link(nc.vector.tensor_reduce(zsum[0:n, :], gate[0:n, :, :], AX_X, ALU.add))
                link(nc.vector.reciprocal(zsum[0:n, :], zsum[0:n, :]))
                link(nc.vector.tensor_tensor(gate[0:n, :, :], gate[0:n, :, :],
                                              zsum[0:n, :].unsqueeze(2).broadcast_to([n, RH, TOPK]), ALU.mult))
                dve.sem_inc(choice_made, 1)
                dve.wait_ge(ct_done, b + 1)
                t = slice(0, n)
                cols = bass.ds(b * P, n)
                nc.vector.tensor_copy(i1T[:, cols], bank(4)[:, 0:n])
                nc.vector.tensor_copy(i2T[:, cols], bank(4)[:, P:P + n])
                link(nc.vector.tensor_copy(ghT[:, cols], bank(4)[:, 2 * P:2 * P + n]))
                nc.vector.tensor_tensor(glT[:, cols], bank(4)[:, 2 * P:2 * P + n], ghT[:, cols].bitcast(F32),
                                        ALU.subtract).then_inc(ct_used, 1)

            for b in range(NB):
                route(b, P if b < SB else NSAM)

            dve.wait_ge(ct_used, NB)
            PER = 4
            with dve.Fori(0, NTOK // UNIT // PER) as i:
                for u in range(PER):
                    dve.wait_ge(g_done, i * PER + (u + 1))
                    for q in range(UNIT):
                        t = bass.ds(i * (PER * UNIT) + (u * UNIT + q), 1)
                        nc.vector.tensor_scalar(O2[u % 2][:, q, :], iota[:, :], i2T[:, t], None, ALU.is_equal)
                        nc.vector.tensor_scalar(A1h[u % 2][:, q, :], iota[:, :], i1T[:, t], ghT[:, t].bitcast(F32),
                                                ALU.is_equal, ALU.mult)
                        ins = nc.vector.tensor_scalar(A1l[u % 2][:, q, :], iota[:, :], i1T[:, t], glT[:, t],
                                                      ALU.is_equal, ALU.mult)
                    ins.then_inc(onehot_made, 1)

            def gated(i, c):
                s = c % 4
                dve.wait_ge(ag_in[s], i * 32 + 32 * (c // 4 + 1))
                nc.vector.tensor_tensor(PA[s][:, :, :], PA[s][:, :, :], PG[s][:, :, :], ALU.mult).then_inc(p_made, 1)

            def gated_lo(i, c):
                s = c % 4
                dve.wait_ge(p_hi_made, i * RING + (c + 1))
                nc.vector.tensor_tensor(P_lo[s][:, :, :], PA[s][:, :, :], P_hi[s][:, :, :].bitcast(F32),
                                        ALU.subtract).then_inc(p_lo_made, 1)

            def add(i, g, d):
                dve.wait_ge(down_done, i * 2 * KT + (KT * g + d + 1))
                dve.wait_ge(y_used, i * 2 * KT + (KT * g + d + 1))
                nc.vector.tensor_tensor(X2[:, d, :, :], pv[d % 2], X2[:, d, :, :], ALU.add).then_inc(y_used, 1)

            def group(i, g, more):
                if more:
                    gated(i, 2 * g + 2)
                    gated(i, 2 * g + 3)
                for d in range(KT):
                    if d == 2 and more:
                        gated_lo(i, 2 * g + 2)
                        gated_lo(i, 2 * g + 3)
                    add(i, g, d)

            for c in range(2):
                gated(0, c)
            for c in range(2):
                gated_lo(0, c)
            with dve.Fori(0, DGROUPS // 2 - 1) as i:
                for g in range(2):
                    group(i, g, True)
            group(0, DGROUPS - 2, True)
            group(0, DGROUPS - 1, False)
            normalise(X2, G_FINAL, 2 * KT, False)


def kernel(**inputs):
    import numpy as np
    import concourse.bacc as bacc
    from concourse.bass_utils import run_bass_kernel_spmd

    a = {k: np.asarray(v) for k, v in inputs.items()}

    def tiles(w):
        return w.reshape(KT, P, -1, P).transpose(2, 1, 0, 3)

    def by_feature(v):
        return v.reshape(-1, KT, P).transpose(2, 0, 1)

    w_in = a["w_in"][0]
    cols = np.cumsum([0, D, D, D, D, H, H, D, D, D, D, D])
    q, k, v, o, ig, fg, cb, cc, cx, ga, gb = (w_in[:, cols[n]:cols[n + 1]] for n in range(11))
    conv = np.stack([tiles(cc), tiles(cx), tiles(cb)], axis=1).reshape(3 * KT, P, KT, P)
    stream = np.concatenate([
        tiles(q), tiles(k), tiles(v), tiles(o), tiles(ga), tiles(a["w_out_a"][0]), conv, tiles(gb),
        tiles(a["w_out_b"][0]), tiles(a["w_o"][0]), tiles(a["w_query"][0]), tiles(a["expert_u"][0].T),
        a["expert_v"][0].reshape(CHUNKS, P, KT, P)])
    wgate = np.zeros((D, P), np.float32)
    wgate[:, 0:H] = ig
    wgate[:, 32:32 + H] = fg
    bif = np.zeros((P, 1), np.float32)
    bif[0:H, 0] = a["b_if"][0][:H]
    bif[32:32 + H, 0] = a["b_if"][0][H:]
    x = np.concatenate([a["x_prompt"].reshape(SEQ, D), a["x_sample"].reshape(NSAM, D)])
    keys = np.stack([a["sub_keys1"][0], a["sub_keys2"][0]], axis=1).reshape(2 * RH, NKEY, P)
    arrays = {
        "x": x.reshape(NTOK, KT, P).transpose(2, 1, 0),
        "wtiles": stream,
        "wgate": tiles(wgate)[0],
        "keysT": keys.transpose(2, 0, 1),
        "c0T": a["state_mlstm_C"][0].transpose(1, 0, 3, 2).reshape(H * NSEQ, HT, P, DH).transpose(0, 2, 1, 3),
        "n0T": a["state_mlstm_n"][0].reshape(NSEQ, H * HT, P).transpose(2, 1, 0),
        "m0": a["state_mlstm_m"][0].T,
        "conv0": a["state_conv"][0].reshape(NSEQ, 2, KT, P).transpose(3, 2, 0, 1),
        "vecs": np.concatenate([by_feature(a["norm_mix"]), by_feature(a["head_norm"][0]), by_feature(a["conv_w"][0]),
                                by_feature(a["norm_ffn"]), by_feature(a["norm_final"])], axis=1),
        "bif": bif,
    }
    arrays = {n: np.ascontiguousarray(t) for n, t in arrays.items()}
    nc = bacc.Bacc("TRN2", target_bir_lowering=False, num_devices=1)
    ins = [nc.dram_tensor(f"in_{n}", t.shape, mybir.dt.from_np(t.dtype), kind="ExternalInput").ap()
           for n, t in arrays.items()]
    outs = {n: nc.dram_tensor(n, s, F32, kind="ExternalOutput").ap() for n, s in OUTS.items()}
    build(nc, *ins, outs)
    r = run_bass_kernel_spmd(nc, [{f"in_{n}": t for n, t in arrays.items()}], core_ids=[0]).results[0]
    y = r["o_y"].transpose(2, 1, 0).reshape(NTOK, D)
    return (
        y[:SEQ].reshape(1, SEQ, D), y[SEQ:].reshape(NSEQ, DSEQ, D),
        r["o_cp"].transpose(0, 3, 2, 1).reshape(1, 1, H, DH, DH),
        r["o_np"].transpose(1, 0).reshape(1, 1, H, DH),
        r["o_mp"].reshape(1, 1, H),
        r["o_convp"].transpose(2, 1, 0).reshape(1, 1, 2, D),
        r["o_cs"].transpose(0, 3, 2, 1).reshape(H, NSEQ, DH, DH).transpose(1, 0, 2, 3)[None],
        r["o_ns"].transpose(2, 1, 0).reshape(1, NSEQ, H, DH),
        r["o_ms"].T[None],
        r["o_convs"].transpose(2, 3, 1, 0).reshape(1, NSEQ, 2, D),
    )
```

```python
from contextlib import ExitStack

import concourse.bass as bass
from concourse import mybir

F32 = mybir.dt.float32
F32R = mybir.dt.float32r
U32 = mybir.dt.uint32
ALU = mybir.AluOpType
ACT = mybir.ActivationFunctionType
AX_X = mybir.AxisListType.X

P = 128
D = 1024
KT = D // P
SEQ = 512
NSEQ, DSEQ = 8, 4
NSAM = NSEQ * DSEQ
NTOK = SEQ + NSAM
HALF = NTOK // 2
H = 4
DH = D // H
HT = DH // P
SB = SEQ // P
NB = SB + 1
RH = 8
NKEY = 128
TOPK = 16
EPS = 1e-6
NEG = -3.0e38
CHUNKS = NKEY

RING = 4
T_Q, T_K, T_V, T_GB, T_GA, T_CONV = (KT * n for n in range(6))
T_WB, T_O, T_WA, T_WO, T_WQ = (T_CONV + KT * n for n in range(3, 8))
T_U = T_WQ + 2 * RH
T_VV = T_U + CHUNKS
T_END = T_VV + CHUNKS
AHEAD = RING - 1

ROUTE_TILES = 12
GTOK = 64
UNIT = 4
UNITS_PER_TILE = 2
GROUPS = SEQ // GTOK
TILES_PER_GROUP = GTOK // (UNIT * UNITS_PER_TILE)
LAST_TILES = NSAM // (UNIT * UNITS_PER_TILE)
GATE_TILES = GROUPS * TILES_PER_GROUP + LAST_TILES
assert NSEQ == UNITS_PER_TILE * RING and H * RING == 2 * KT
assert NB * ROUTE_TILES + GATE_TILES == CHUNKS and GATE_TILES % RING == 0 and ROUTE_TILES % RING == 0
DGROUPS = CHUNKS // 2

OUTS = {
    "o_y": (P, KT, NTOK), "o_cp": (H, P, HT, DH), "o_np": (P, H * HT), "o_mp": (H, 1),
    "o_convp": (P, KT, 2), "o_cs": (H * NSEQ, P, HT, DH), "o_ns": (P, H * HT, NSEQ),
    "o_ms": (H, NSEQ), "o_convs": (P, KT, NSEQ, 2),
}


def build(nc, x, wtiles, wgate, keysT, c0T, n0T, m0, conv0, vecs, bif, outs):
    ctx = ExitStack()
    with ctx:
        def sem(name):
            return ctx.enter_context(nc.semaphore(name))

        A = KT * NTOK * 4
        base = (nc.sbuf_base + 63) // 64 * 64
        at = {"p": base}

        def put(name, shape, dt=F32, offset=None):
            size = 4
            for s in shape[1:]:
                size *= s
            if offset is None:
                offset = at["p"]
                at["p"] += (size + 31) // 32 * 32
            return nc.alloc_sbuf_tensor_at(name, list(shape), dt, offset=offset)

        w_raw = [put(f"w_raw{r}", [P, KT, P]) for r in range(RING)]
        w_hi = [put(f"w_hi{r}", [P, KT, P], F32R) for r in range(RING)]
        w_lo = [put(f"w_lo{r}", [P, KT, P], F32R) for r in range(RING)]
        ident = put("ident", [P, P])
        ones = put("ones", [P, P])
        causal = put("causal", [P, P])
        iota = put("iota", [P, P])
        iota16 = put("iota16", [P, TOPK])
        sel = put("sel", [H, H, P])
        sam_mask = put("sam_mask", [NSAM, NSEQ, DSEQ])
        seq_mask = put("seq_mask", [NSAM, NSEQ])
        vec = put("vec", [P, 7, KT])
        G_MIX, G_HEAD, G_CONV, G_FFN, G_FINAL = 0, 1, 2, 5, 6
        bias_if = put("bias_if", [P, 1])
        m0_sb = put("m0_sb", [H, NSEQ])
        conv0_sb = put("conv0_sb", [P, KT, NSEQ, 2])
        convp_sb = put("convp_sb", [P, KT, 2])
        convs_sb = put("convs_sb", [P, KT, NSEQ, 2])
        n0_sb = put("n0_sb", [P, H * HT, NSEQ])
        np_sb = put("np_sb", [P, H * HT])
        ns_sb = put("ns_sb", [P, H * HT, NSEQ])
        a_col = put("a_col", [P, NB, H])
        dec_col = put("dec_col", [P, NB, H])
        eps_col = put("eps_col", [P, 1])
        ms_sb = put("ms_sb", [H, NSEQ])
        mp_sb = put("mp_sb", [H, 1])
        R0 = (at["p"] + 63) // 64 * 64
        R = [R0 + k * A for k in range(8)]
        T0 = R0 + 8 * A
        TSIZE = nc.sbuf_usable_end - T0
        L0 = R[7] + 2 * D * 4

        def act_buf(name, k, dt=F32):
            return put(name, [P, KT, 2, HALF], dt, R[k])

        def flat(t):
            return t[:, :, :, :].rearrange("p k a b -> p k (a b)")

        X = act_buf("x_in", 0)
        H_hi, H_lo = act_buf("h_hi", 1, F32R), act_buf("h_lo", 2, F32R)
        Q, K = act_buf("q", 3), act_buf("k", 4)
        VT = act_buf("v_feature", 0)
        HN = act_buf("hn", 0)
        K_tok = put("k_tok", [P, SB, D], F32, R[5])
        V_tok = put("v_tok", [P, SB, D], F32, R[5] + SB * D * 4)
        assert 2 * SB * D * 4 + HT * DH * 4 <= 2 * A
        k_sam = put("k_sam", [P, D], F32, R[7])
        v_sam = put("v_sam", [P, D], F32, R[7] + D * 4)
        S_hi, S_lo = act_buf("s_hi", 3, F32R), act_buf("s_lo", 4, F32R)
        SG = put("sg", [P, 2 * KT, 2, HALF], F32, R[5])
        M1 = SG
        M_hi = act_buf("m_hi", 7, F32R)
        M_lo = H_hi
        X_again = act_buf("x_again", 2)
        X2 = act_buf("x2", 0)
        sq_ffn, sq_final = act_buf("sq_ffn", 3), act_buf("sq_final", 1)

        sq = [put(f"sq{n}", [P, 2, HALF], F32, T0 + n * 2176) for n in range(2)]
        rs = put("rs", [P, 2, HALF], F32, T0 + 2 * 2176)
        ht = [put(f"ht{n}", [P, 2, HALF], F32, T0 + (3 + n) * 2176) for n in range(2)]
        wg_raw = put("wg_raw", [P, KT, P], F32, T0 + 5 * 2176)
        wg_hi = put("wg_hi", [P, KT, P], F32R, R[3])
        wg_lo = put("wg_lo", [P, KT, P], F32R, R[3] + 4096)
        GB = R[5]
        grow = [put(f"grow{n}", [64, NTOK], F32, GB + n * 2176) for n in range(12)]
        M_row = put("m_stab", [H, NTOK], F32, T0)
        E_row = put("e_row", [H, NTOK], F32, T0 + 2176)
        W = [put(f"w_sc{n}", [P, SB * SEQ - P * (SB * (SB - 1) // 2)], F32, T0 + 4352 + n * 5120)
             for n in range(2)]
        dV = put("dV", [P, SB, DH], F32, L0)
        C_out = put("c_out", [P, HT, DH], F32, R[5] + 2 * SB * D * 4)
        r_buf = put("r_buf", [P, SEQ], F32, L0 + 4096)
        hsq = [put("hsq0", [P, SEQ], F32, L0 + 6144), put("hsq1", [P, SEQ], F32, T0 + 4352 + 10240 + 128)]
        STR = 4
        c0_ring = [put(f"c0_ring{n}", [P, HT, DH], F32, L0 + n * 2048) for n in range(STR)]
        cn_ring = [put(f"cn_ring{n}", [P, HT, DH], F32, T0 + 4352 + 5248 + n * 2048) for n in range(STR)]
        assert 4352 + 5248 + STR * 2048 <= TSIZE and 2 * D * 4 + STR * 2048 <= A
        km = [put(f"km{n}", [P, DH], F32, T0 + n * 1024) for n in range(2)]
        s_small = T0 + 4352
        Ws = put("ws", [NSAM, H, NSAM], F32, s_small)
        alpha_s = put("alpha_s", [P, H, NSAM], F32, s_small + 512)
        q_al = put("q_al", [P, H * HT, NSAM], F32, s_small + 1024)
        qn = put("qn", [P, H * HT, NSAM], F32, s_small + 2048)
        dm = put("dm", [P, H, NSEQ], F32, s_small + 3072)
        rsam = put("rsam", [P, H, NSAM], F32, s_small + 3200)
        sqs = put("sqs", [P, H * HT, NSAM], F32, s_small + 3712)
        rss = put("rss", [P, H, NSAM], F32, s_small + 4736)
        al_row = put("al_row", [H, NSAM], F32, T0 + 4352 + 10240)
        tmp = [put(f"tmp{n}", [P, 2, HALF], F32, T0 + n * 2176) for n in range(2)]
        cc_t = put("cc_t", [P, 2, HALF], F32, T0 + 2 * 2176)
        so_t = [put(f"so_t{n}", [P, 2, HALF], F32, T0 + (2 + n) * 2176) for n in range(2)]
        u_t = put("u_t", [P, 2, HALF], F32, T0 + 3 * 2176)
        y_t = put("y_t", [P, 2, HALF], F32, T0 + 4 * 2176)
        ext = put("ext", [P, NSEQ, 2 + DSEQ], F32, T0 + 5 * 2176)
        qT = [put(f"qT{n}", [P, 2, HALF], F32, T0 + n * 2176) for n in range(2)]
        keys_sb = put("keys_sb", [P, 2 * RH, NKEY], F32, R[6])
        S_all = put("s_all", [P, NB, 2 * RH, NKEY], F32, R[3])
        o = R[3] + NB * 2 * RH * NKEY * 4
        S_blk = put("s_blk", [P, 2 * RH, NKEY], F32, o)
        cand = put("cand", [P, RH, TOPK, TOPK], F32, o + 8192)
        eq = put("eq", [P, RH, TOPK, TOPK], F32, o + 2 * 8192)
        pr = put("pr", [P, RH, TOPK, TOPK], F32, o + 3 * 8192)
        assert o + 4 * 8192 <= R[3] + 77824
        A_ring = [put(f"a_ring{n}", [P, 2, HALF], F32, T0 + n * 2176) for n in range(4)]
        t1 = T0 + 4 * 2176
        small = {}
        for name, shape, dt in (
            ("val", [P, 2 * RH, TOPK], F32), ("ind", [P, 2 * RH, TOPK], U32), ("indf", [P, 2 * RH, TOPK], F32),
            ("best", [P, RH, TOPK], F32), ("pos", [P, RH, TOPK], U32), ("posw", [P, RH, TOPK], U32),
            ("posf", [P, RH, TOPK], F32), ("e1", [P, RH, TOPK], F32), ("e2", [P, RH, TOPK], F32),
            ("gate", [P, RH, TOPK], F32), ("zsum", [P, RH], F32),
        ):
            small[name] = put(name, shape, dt, t1)
            t1 += shape[1] * (shape[2] if len(shape) > 2 else 1) * 4
        assert t1 <= nc.sbuf_usable_end
        G_st = [put(f"g_st{n}", [P, NKEY, GTOK], F32, R[3] + n * 32768) for n in range(2)]
        oh = R[3] + 65536
        O2 = [put(f"o2_{n}", [P, UNIT, NKEY], F32, oh + n * 4096) for n in range(2)]
        A1 = [put(f"a1_{n}", [P, UNIT, NKEY], F32, oh + n * 4096 + 2048) for n in range(2)]
        ch = R[3] + 77824
        i1T = put("i1T", [P, NTOK], F32, ch)
        i2T = put("i2T", [P, NTOK], F32, ch + 2176)
        gT = put("gT", [P, NTOK], F32, ch + 2 * 2176)
        assert ch + 3 * 2176 <= R[3] + 5 * A
        PA = [put(f"pa{n}", [P, 2, HALF], F32, R[3] + n * 2176) for n in range(4)]
        PG = [put(f"pg{n}", [P, 2, HALF], F32, R[3] + (4 + n) * 2176) for n in range(4)]
        P_hi = [put(f"p_hi{n}", [P, 2, HALF], F32R, R[4] + n * 2176) for n in range(4)]
        P_lo = [put(f"p_lo{n}", [P, 2, HALF], F32R, R[4] + (4 + n) * 2176) for n in range(4)]
        assert TSIZE >= 15 * 1024, TSIZE

        A_dram = nc.dram_tensor("a_scratch", (CHUNKS, P, NTOK), F32).ap()
        G_dram = nc.dram_tensor("g_scratch", (CHUNKS, P, NTOK), F32).ap()

        pair = [ctx.enter_context(nc.psum_tensor(f"pair{n}", [P, 1024], F32)) for n in range(4)]
        pv = [t[:, :].rearrange("p (a b) -> p a b", a=2)[:, :, 0:HALF] for t in pair]

        def bank(n):
            return pair[n // 2][:, 512 * (n % 2):512 * (n % 2) + 512]

        x_in = [sem(f"x_loaded{k}") for k in range(KT)]
        consts_in = sem("consts_loaded")
        wg_in = sem("gate_weights_loaded")
        raw_in = [sem(f"raw_loaded{r}") for r in range(RING)]
        hi_made = sem("weights_hi_made")
        lo_made = sem("weights_lo_made")
        tile_done = sem("tile_done")
        out_used = sem("out_used")
        masks_step, masks_made = sem("masks_step"), sem("masks_made")
        sq_made, sq_used, ssq_done, std_made = sem("sq_made"), sem("sq_used"), sem("ssq_done"), sem("std_made")
        ht_made, hh_made, hl_made = sem("ht_made"), sem("hh_made"), sem("hl_made")
        wg_hi_made, wg_lo_made, gate_done = sem("wg_hi_made"), sem("wg_lo_made"), sem("gate_done")
        gate_act = sem("gate_act")
        gate_neg = sem("gate_neg")
        rows_made = sem("rows_made")
        row_args = sem("row_args")
        dve_chain = sem("dve_chain")
        act_chain = sem("act_chain")
        tr_done, tr_k_used, tr_v_used = sem("tr_done"), sem("tr_k_used"), sem("tr_v_used")
        cols_done, cols_used = sem("cols_done"), sem("cols_used")
        s_done, w_arg, w_exp, sw_made = sem("s_done"), sem("w_arg"), sem("w_exp"), sem("sw_made")
        num_done, abs_made, hout_made = sem("num_done"), sem("abs_made"), sem("hout_made")
        m_done, e_used, n_done = sem("m_done"), sem("e_used"), sem("n_done")
        hsq_made, hsq_used, hstd_made = sem("hsq_made"), sem("hsq_used"), sem("hstd_made")
        head_done, dv_made, st_done = sem("head_done"), sem("dv_made"), sem("st_done")
        cout_made, cout_stored, n_used = sem("cout_made"), sem("cout_stored"), sem("n_used")
        sam_zero = sem("sam_zero")
        sb_done, sam_al, sam_arg, sam_exp, sam_sw = (sem("sam_bcast_done"), sem("sam_alpha"), sem("sam_arg"),
                                                     sem("sam_exp"), sem("sam_sw"))
        c0_in = [sem(f"c0_in{n}") for n in range(STR)]
        upd_done, cn_made = sem("upd_done"), sem("cn_made")
        cn_stored = [sem(f"cn_stored{n}") for n in range(STR)]
        km_made, sam_num = sem("km_made"), sem("sam_num")
        sam_abs, sam_hout, sam_sq, sam_rms, sam_std, sam_hn = (sem("sam_abs"), sem("sam_hout"), sem("sam_sq"),
                                                               sem("sam_rms"), sem("sam_std"), sem("sam_hn"))
        t_made, t_hi, t_lo = sem("t_made"), sem("t_hi"), sem("t_lo")
        cc_used = sem("cc_used")
        xa_in = sem("x_again_loaded")
        keys_in = sem("keys_loaded")
        sc_done, sc_used = sem("scores_done"), sem("scores_used")
        blk_made, blk_used = sem("block_copied"), sem("block_used")
        sm_arg, sm_exp, choice_made = sem("softmax_arg"), sem("softmax_exp"), sem("choice_made")
        ct_done, ct_used = sem("choice_turned"), sem("choice_kept")
        onehot_made, g_done, g_used = sem("onehot_made"), sem("gate_units_done"), sem("gate_units_used")
        g_stored = [sem(f"g_stored{n}") for n in range(2)]
        a_stored = [sem(f"a_stored{n}") for n in range(4)]
        ag_in = [sem(f"ag_in{n}") for n in range(4)]
        p_made, p_hi_made, p_lo_made = sem("p_made"), sem("p_hi_made"), sem("p_lo_made")
        down_done, y_used = sem("down_done"), sem("y_used")
        y_made, stored = sem("y_made"), sem("stored")

        block = ctx.enter_context(nc.Block())

        @block.sync
        def _(sp):
            for k in range(KT):
                sp.dma_start(flat(X)[:, k, :], x[:, k, :]).then_inc(x_in[k], 16)
            for dst, src in ((vec[:, :, :], vecs), (bias_if[:, :], bif), (m0_sb[:, :], m0),
                             (conv0_sb[:, :, :, :], conv0), (n0_sb[:, :, :], n0T)):
                sp.dma_start(dst, src).then_inc(consts_in, 16)
            sp.dma_start(wg_raw[:, :, :], wgate).then_inc(wg_in, 16)

            def load_tile(group, r):
                sp.dma_start(w_raw[r][:, :, :], wtiles[group * RING + r]).then_inc(raw_in[r], 16)

            def load_tiles(first, last):
                with sp.Fori(first, last) as i:
                    for r in range(RING):
                        sp.wait_ge(lo_made, i * RING + (r - RING + 1))
                        load_tile(i, r)

            for r in range(RING):
                load_tile(0, r)
            load_tiles(1, (T_GB + RING) // RING)

            sp.wait_ge(st_done, H)
            sp.wait_ge(hsq_used, H * HT)
            sp.wait_ge(head_done, H)

            def load_c0(i, u):
                sp.dma_start(c0_ring[u % STR][:, :, :], c0T[i * NSEQ + u]).then_inc(c0_in[u % STR], 16)

            def states(i, last):
                for r in range(RING):
                    sp.wait_ge(lo_made, i * RING + (T_GB + r + 1))
                    load_tile(i + (T_GB // RING + 1), r)
                    for u in range(UNITS_PER_TILE * r, UNITS_PER_TILE * (r + 1)):
                        sp.wait_ge(cn_made, i * NSEQ + (u + 3))
                        sp.dma_start(outs["o_cs"][i * NSEQ + u], cn_ring[u % STR][:, :, :]).then_inc(cn_stored[u % STR], 16)
                        if not last or u + STR < NSEQ:
                            load_c0(i, u + STR)

            for u in range(STR):
                load_c0(0, u)
            with sp.Fori(0, H - 1) as i:
                states(i, False)
            states(H - 1, True)
            load_tiles((T_CONV + RING) // RING, (T_WA + RING) // RING)
            sp.wait_ge(out_used, T_WA + 2)
            sp.dma_start(flat(X_again), x).then_inc(xa_in, 16)
            load_tiles((T_WA + RING) // RING, (T_WO + RING) // RING)
            sp.wait_ge(t_lo, KT * 3)
            sp.dma_start(keys_sb[:, :, :], keysT).then_inc(keys_in, 16)
            load_tiles((T_WO + RING) // RING, (T_VV + RING) // RING)

            for n in range(4):
                sp.wait_ge(a_stored[n], 16 * (CHUNKS // 4))
            for n in range(2):
                sp.wait_ge(g_stored[n], 16 * (GROUPS // 2 + (1 - n)))

            def load_ag(c, s):
                sp.dma_start(PA[s][:, :, :].rearrange("p a b -> p (a b)"), A_dram[c]).then_inc(ag_in[s], 16)
                sp.dma_start(PG[s][:, :, :].rearrange("p a b -> p (a b)"), G_dram[c]).then_inc(ag_in[s], 16)

            for s in range(4):
                load_ag(s, s)
            with sp.Fori(1, CHUNKS // 4) as i:
                for s in range(4):
                    sp.wait_ge(lo_made, i * RING + (T_VV + s - RING + 1))
                    sp.dma_start(w_raw[s][:, :, :], wtiles[i * RING + (T_VV + s)]).then_inc(raw_in[s], 16)
                    sp.wait_ge(p_lo_made, i * 4 + (s - 3))
                    load_ag(i * 4 + s, s)
            n_out = 0
            for name, src, ready, count in (
                ("o_np", np_sb[:, :], n_used, H), ("o_mp", mp_sb[:, :], rows_made, 1),
                ("o_ms", ms_sb[:, :], rows_made, 1), ("o_ns", ns_sb[:, :, :], sam_hn, 1),
                ("o_convp", convp_sb[:, :, :], t_lo, KT), ("o_convs", convs_sb[:, :, :, :], t_lo, KT),
            ):
                sp.wait_ge(ready, count)
                sp.dma_start(outs[name], src).then_inc(stored, 16)
                n_out += 1
            for k in range(KT):
                sp.wait_ge(y_made, k + 1)
                sp.dma_start(outs["o_y"][:, k, :], X2[:, k, :, :].rearrange("p a b -> p (a b)")).then_inc(stored, 16)
                n_out += 1
            sp.wait_ge(stored, 16 * n_out)
            for n in range(STR):
                sp.wait_ge(cn_stored[n], 16 + 16 * (H * NSEQ // STR))
            sp.wait_ge(cout_stored, 16 * H)

        @block.gpsimd
        def _(pool):
            pool.memset(ones[:, :], 1.0).then_inc(masks_step, 1)
            pool.memset(ident[:, :], 0.0).then_inc(masks_step, 1)
            pool.memset(causal[:, :], 1.0).then_inc(masks_step, 1)
            pool.memset(sel[:, :, :], 0.0).then_inc(masks_step, 1)
            pool.memset(sam_mask[:, :, :], 1.0).then_inc(masks_step, 1)
            pool.memset(seq_mask[:, :], 1.0).then_inc(masks_step, 1)
            pool.memset(eps_col[:, :], EPS).then_inc(masks_step, 1)
            pool.iota(iota[:, :], [[1, NKEY]], base=0, channel_multiplier=0,
                      allow_small_or_imprecise_dtypes=True).then_inc(masks_step, 1)
            pool.iota(iota16[:, :], [[1, TOPK]], base=0, channel_multiplier=0,
                      allow_small_or_imprecise_dtypes=True).then_inc(masks_step, 1)
            pool.wait_ge(masks_step, 9)
            pool.affine_select(out=ident[:, :], in_=ident[:, :], compare_op=ALU.not_equal, fill=1.0,
                               base=0, pattern=[[-1, P]], channel_multiplier=1).then_inc(masks_step, 1)
            pool.affine_select(out=causal[:, :], in_=causal[:, :], compare_op=ALU.is_ge, fill=0.0,
                               base=0, pattern=[[1, P]], channel_multiplier=-1).then_inc(masks_step, 1)
            pool.affine_select(out=sel[:, :, :], in_=sel[:, :, :], compare_op=ALU.not_equal, fill=1.0,
                               base=0, pattern=[[-1, H], [0, P]], channel_multiplier=1).then_inc(masks_step, 1)
            pool.affine_select(out=sam_mask[:, :, :], in_=sam_mask[:, :, :], compare_op=ALU.is_ge, fill=0.0,
                               base=0, pattern=[[DSEQ, NSEQ], [1, DSEQ]], channel_multiplier=-1).then_inc(masks_step, 1)
            pool.affine_select(out=seq_mask[:, :], in_=seq_mask[:, :], compare_op=ALU.is_ge, fill=0.0,
                               base=0, pattern=[[-DSEQ, NSEQ]], channel_multiplier=1).then_inc(masks_step, 1)
            pool.wait_ge(masks_step, 14)
            pool.affine_select(out=sam_mask[:, :, :], in_=sam_mask[:, :, :], compare_op=ALU.is_ge, fill=0.0,
                               base=0, pattern=[[-DSEQ, NSEQ], [0, DSEQ]], channel_multiplier=1).then_inc(masks_made, 1)
            pool.affine_select(out=seq_mask[:, :], in_=seq_mask[:, :], compare_op=ALU.is_ge, fill=0.0,
                               base=DSEQ - 1, pattern=[[DSEQ, NSEQ]], channel_multiplier=-1).then_inc(masks_made, 1)

            with pool.Fori(0, T_END // RING) as i:
                for r in range(RING):
                    pool.wait_ge(hi_made, i * RING + (r + 1))
                    nc.gpsimd.tensor_tensor(w_lo[r][:, :, :], w_raw[r][:, :, :], w_hi[r][:, :, :].bitcast(F32),
                                            ALU.subtract).then_inc(lo_made, 1)

        @block.tensor
        def _(pe):
            def project(i, t, hi, lo, before=None, after=None):
                r, out = t % RING, pair[t % 2]
                pe.wait_ge(lo_made, i * RING + (t + 1))
                pe.wait_ge(out_used, i * RING + (t + 1))
                for k in range(KT):
                    if before is not None:
                        before(k)
                    for w, xs in ((w_hi, (hi, lo)), (w_lo, (hi,))):
                        for x_part in xs:
                            for a in range(2):
                                mm = nc.tensor.matmul(out[:, 512 * a:512 * a + HALF], w[r][:, k, :],
                                                      x_part[:, k, a, :], start=(k == 0 and w is w_hi and x_part is hi),
                                                      stop=(k == KT - 1 and w is w_lo))
                    if k == KT - 1:
                        mm.then_inc(tile_done, 1)
                    if after is not None:
                        after(k)

            def project_all(t0, n, hi, lo, ready=None):
                if ready is not None:
                    for r in range(RING):
                        project(0, t0 + r, hi, lo, before=lambda k: r == 0 and pe.wait_ge(ready[0], ready[1] + k + 1))
                with pe.Fori(0 if ready is None else 1, n // RING) as i:
                    for r in range(RING):
                        project(i, t0 + r, hi, lo)

            def sum_squares(base, out, part):
                for k in range(KT):
                    pe.wait_ge(sq_made, base + k + 1)
                    for a in range(2):
                        mm = nc.tensor.matmul(out[:, 512 * a:512 * a + HALF], ones[:, :], part(k)[:, a, :],
                                              start=(k == 0), stop=(k == KT - 1))
                    mm.then_inc(sq_used, 1)

            pe.wait_ge(masks_made, 2)
            sum_squares(0, pair[0], lambda k: sq[k % 2])
            pe.wait_ge(wg_lo_made, 1)
            for k in range(KT):
                pe.wait_ge(hl_made, k + 1)
                for w, xs in ((wg_hi, (H_hi, H_lo)), (wg_lo, (H_hi,))):
                    for x_part in xs:
                        for a in range(2):
                            mm = nc.tensor.matmul(pair[1][:, 512 * a:512 * a + HALF], w[:, k, :], x_part[:, k, a, :],
                                                  start=(k == 0 and w is wg_hi and x_part is H_hi),
                                                  stop=(k == KT - 1 and w is wg_lo))
            mm.then_inc(gate_done, 1)
            project_all(T_Q, KT, H_hi, H_lo)
            project_all(T_K, KT, H_hi, H_lo)
            pe.wait_ge(rows_made, 1)
            for b in range(NB):
                n = P if b < SB else NSAM
                for j, row in enumerate((grow[0], grow[1])):
                    mm = nc.tensor.matmul(bank(4)[0:n, (2 * b + j) * H:(2 * b + j + 1) * H], row[0:H, b * P:b * P + n],
                                          ident[0:H, 0:H], start=True, stop=True)
            mm.then_inc(cols_done, 1)
            project_all(T_V, KT, H_hi, H_lo)

            pe.wait_ge(out_used, T_V + KT + 2)
            pe.wait_ge(cols_used, 1)
            units = [(src, b, q) for b in range(NB) for q in range(2) for src in (0, 1)]
            for n, (src, b, q) in enumerate(units):
                if n >= 4:
                    m = (n - 4) // 2 + 1
                    pe.wait_ge(tr_v_used if src else tr_k_used, m)
                rows = P if b < SB else NSAM
                for j in range(4):
                    mm = nc.tensor.transpose(bank(4 + n % 4)[0:rows, j * P:(j + 1) * P],
                                             flat(VT if src else K)[:, 4 * q + j, b * P:b * P + rows], ident[:, :])
                mm.then_inc(tr_done, 1)
            pe.wait_ge(tr_k_used, 2 * NB)
            pe.wait_ge(tr_v_used, 2 * NB)

            off = [0, 512, 1024, 896]

            def stabiliser(h):
                mm = nc.tensor.matmul(bank(3), sel[0:H, h, :], M_row[:, 0:SEQ], start=True, stop=True)
                mm.then_inc(m_done, 1)

            def head_scores(h):
                for s in range(SB):
                    n = SEQ - s * P
                    dst = bank(off[s] // 512)[:, off[s] % 512:off[s] % 512 + n]
                    for k in range(HT):
                        mm = nc.tensor.matmul(dst, flat(K)[:, h * HT + k, s * P:s * P + P],
                                              flat(Q)[:, h * HT + k, s * P:SEQ], start=(k == 0), stop=(k == HT - 1))
                mm.then_inc(s_done, 1)

            stabiliser(0)
            head_scores(0)
            for h in range(H):
                pe.wait_ge(w_arg, SB * (h + 1))
                nc.tensor.matmul(bank(3), sel[0:H, h, :], E_row[:, 0:SEQ], start=True, stop=True)
                pe.wait_ge(sw_made, h + 1)
                if h:
                    pe.wait_ge(hout_made, 2 * h)
                    pe.wait_ge(hstd_made, h)
                w_off = 0
                for s in range(SB):
                    n = SEQ - s * P
                    sw = W[h % 2][:, w_off:w_off + n]
                    w_off += n
                    for v in range(HT):
                        nc.tensor.matmul(bank(5 + v)[:, s * P:SEQ], V_tok[:, s, h * DH + v * P:h * DH + (v + 1) * P], sw,
                                         start=(s == 0), stop=(s == SB - 1))
                    mm = nc.tensor.matmul(bank(7)[:, s * P:SEQ], ones[:, :], sw, start=(s == 0), stop=(s == SB - 1))
                mm.then_inc(num_done, 1)
                if h + 1 < H:
                    head_scores(h + 1)
                    pe.wait_ge(e_used, h + 1)
                    stabiliser(h + 1)
                pe.wait_ge(abs_made, h + 1)
                for k in range(HT):
                    for s in range(SB):
                        kt = K_tok[:, s, h * DH + k * P:h * DH + (k + 1) * P]
                        mm = nc.tensor.matmul(bank(7)[:, k:k + 1], kt, dec_col[:, s, h:h + 1],
                                              start=(s == 0), stop=(s == SB - 1))
                mm.then_inc(n_done, 1)
                pe.wait_ge(dv_made, h + 1)
                if h:
                    pe.wait_ge(cout_made, h)
                for k in range(HT):
                    for s in range(SB):
                        kt = K_tok[:, s, h * DH + k * P:h * DH + (k + 1) * P]
                        mm = nc.tensor.matmul(bank(4)[:, k * DH:(k + 1) * DH], kt, dV[:, s, :],
                                              start=(s == 0), stop=(s == SB - 1))
                mm.then_inc(st_done, 1)
                pe.wait_ge(n_used, h + 1)
                for v in range(HT):
                    pe.wait_ge(hsq_made, HT * h + v + 1)
                    mm = nc.tensor.matmul(bank(7), ones[:, :], hsq[v][:, :], start=(v == 0), stop=(v == HT - 1))
                    mm.then_inc(hsq_used, 1)

            pe.wait_ge(cout_made, H)
            pe.wait_ge(n_used, H)
            pe.wait_ge(hstd_made, H)
            pe.wait_ge(hout_made, 2 * H)
            for h in range(H):
                nc.tensor.matmul(bank(0)[0:NSAM, P + h * NSAM:P + (h + 1) * NSAM], sel[0:H, h, 0:NSAM],
                                 M_row[:, SEQ:NTOK], start=True, stop=True)
                nc.tensor.matmul(bank(1)[:, h * NSAM:(h + 1) * NSAM], sel[0:H, h, :], al_row[:, :], start=True, stop=True)
                nc.tensor.matmul(bank(4)[:, 2 * P + h * NSAM:2 * P + (h + 1) * NSAM], sel[0:H, h, :], E_row[:, SEQ:NTOK],
                                 start=True, stop=True)
            for h in range(H):
                for k in range(HT):
                    mm = nc.tensor.matmul(bank(0)[0:NSAM, h * NSAM:(h + 1) * NSAM], flat(K)[:, h * HT + k, SEQ:NTOK],
                                          flat(Q)[:, h * HT + k, SEQ:NTOK], start=(k == 0), stop=(k == HT - 1))
            mm.then_inc(sb_done, 1)
            pe.wait_ge(sam_sw, 1)
            for h in range(H):
                nc.tensor.matmul(bank(4)[:, h * NSAM:(h + 1) * NSAM], ones[0:NSAM, :], Ws[:, h, :], start=True, stop=False)
                for k in range(HT):
                    nc.tensor.matmul(bank(4)[:, h * NSAM:(h + 1) * NSAM], ones[:, :], qn[:, h * HT + k, :],
                                     start=False, stop=(k == HT - 1))
            for h in range(H):
                for k in range(HT):
                    mm = nc.tensor.matmul(bank(4)[:, P + (h * HT + k) * NSEQ:P + (h * HT + k + 1) * NSEQ],
                                          k_sam[0:NSAM, h * DH + k * P:h * DH + (k + 1) * P], dm[0:NSAM, h, :],
                                          start=True, stop=True)
            for h in range(H):
                for v in range(HT):
                    nc.tensor.matmul(bank(5)[:, (h * HT + v) * NSAM:(h * HT + v + 1) * NSAM],
                                     v_sam[0:NSAM, h * DH + v * P:h * DH + (v + 1) * P], Ws[:, h, :],
                                     start=(h == 0 and v == 0), stop=False, skip_group_check=True)
            pe.sem_inc(upd_done, 2)
            pe.wait_ge(sam_al, 1)

            def state_unit(i, u):
                pe.wait_ge(c0_in[u % STR], i * (16 * (NSEQ // STR)) + 16 * (u // STR + 1))
                q_flat = q_al[:, :, :].rearrange("p f t -> p (f t)")
                for v in range(HT):
                    for k in range(HT):
                        mm = nc.tensor.matmul(bank(5)[:, bass.ds(i * (HT * NSAM) + (v * NSAM + u * DSEQ), DSEQ)],
                                              c0_ring[u % STR][:, k, v * P:(v + 1) * P],
                                              q_flat[:, bass.ds(i * (HT * NSAM) + (k * NSAM + u * DSEQ), DSEQ)],
                                              start=False, stop=(k == HT - 1), skip_group_check=True)
                mm.then_inc(sam_num, 1)
                pe.wait_ge(km_made, i * NSEQ + (u + 1))
                pe.wait_ge(cn_made, i * NSEQ + (u + 1))
                for k in range(HT):
                    mm = nc.tensor.matmul(bank(6 + u % 2)[:, k * DH:(k + 1) * DH], km[u % 2][:, k * P:(k + 1) * P],
                                          v_sam[:, bass.ds(i * DH, DH)], start=True, stop=True)
                mm.then_inc(upd_done, 1)

            with pe.Fori(0, H) as i:
                for r in range(RING):
                    def after(k):
                        u, rest = divmod(k + 1, KT // UNITS_PER_TILE)
                        if rest == 0:
                            state_unit(i, UNITS_PER_TILE * r + u - 1)
                    project(i, T_GB + r, H_hi, H_lo, after=after)

            for r in range(RING):
                project(0, T_CONV + r, H_hi, H_lo)
                if r == 0:
                    pe.wait_ge(sam_sq, 1)
                    for h in range(H):
                        for v in range(HT):
                            mm = nc.tensor.matmul(bank(4)[:, 3 * P + h * NSAM:3 * P + (h + 1) * NSAM], ones[:, :],
                                                  sqs[:, h * HT + v, :], start=(v == 0), stop=(v == HT - 1))
                    mm.then_inc(sam_rms, 1)
            project_all(T_CONV + RING, 3 * KT - RING, H_hi, H_lo)
            project_all(T_WB, KT, S_hi, S_lo, (t_lo, 0))
            project_all(T_O, KT, H_hi, H_lo)
            project_all(T_WA, KT, S_hi, S_lo, (t_lo, KT))
            project_all(T_WO, KT, M_hi, M_lo, (t_lo, 2 * KT))
            sum_squares(KT, pair[2], lambda k: sq_ffn[:, k, :, :])
            pe.wait_ge(out_used, T_WQ + 2)

            def scores(i, j):
                out = pair[2 + j % 2]
                pe.wait_ge(out_used, i * RING + (T_WQ + j + 3))
                pe.wait_ge(sc_used, i * RING + (j + 1))
                for b in range(NB):
                    n = P if b < SB else NSAM
                    mm = nc.tensor.matmul(out[0:n, b * P:(b + 1) * P],
                                          qT[j % 2][:, :, :].rearrange("p a b -> p (a b)")[:, b * P:b * P + n],
                                          keys_sb[:, i * RING + j, :], start=True, stop=True)
                mm.then_inc(sc_done, 1)

            pe.sem_inc(sc_done, 2)
            pe.sem_inc(g_done, 2)
            pe.wait_ge(keys_in, 16)
            for r in range(RING):
                project(0, T_WQ + r, H_hi, H_lo, before=lambda k: r == 0 and pe.wait_ge(hl_made, KT + k + 1))
                if r:
                    scores(0, r - 1)
            with pe.Fori(1, 2 * RH // RING) as i:
                for r in range(RING):
                    project(i, T_WQ + r, H_hi, H_lo)
                    scores(i, r - 1)
            scores(0, 2 * RH - 1)

            pe.wait_ge(sc_used, 2 * RH + 2)

            def up_and_turn(b, n):
                for r in range(ROUTE_TILES):
                    project(b * (ROUTE_TILES // RING), T_U + r, H_hi, H_lo)
                pe.wait_ge(choice_made, b + 1)
                if not (isinstance(b, int) and b == 0):
                    pe.wait_ge(ct_used, b)
                for j, src in enumerate((small["e1"], small["e2"], small["gate"])):
                    mm = nc.tensor.transpose(bank(4)[:, j * P:j * P + n],
                                             src[0:n, :, :].rearrange("p h k -> p (h k)"), ident[0:n, 0:n])
                mm.then_inc(ct_done, 1)

            up_and_turn(0, P)
            with pe.Fori(1, SB) as b:
                up_and_turn(b, P)
            up_and_turn(SB, NSAM)

            def gate_unit(i, per, u):
                pe.wait_ge(onehot_made, i * per + (u + 1))
                pe.wait_ge(g_used, i * per + (u + 1))
                for q in range(UNIT):
                    mm = nc.tensor.matmul(bank(4 + u % 4)[:, q * NKEY:(q + 1) * NKEY], O2[u % 2][:, q, :],
                                          A1[u % 2][:, q, :], start=True, stop=True)
                mm.then_inc(g_done, 1)

            t0 = T_U + NB * ROUTE_TILES

            def up_and_gate(i, r):
                def after(k):
                    u, rest = divmod(k + 1, KT // UNITS_PER_TILE)
                    if rest == 0:
                        gate_unit(i, RING * UNITS_PER_TILE, UNITS_PER_TILE * r + u - 1)
                project(i, t0 + r, H_hi, H_lo, after=after)

            with pe.Fori(0, GATE_TILES // RING) as i:
                for r in range(RING):
                    up_and_gate(i, r)

            def down(i, g):
                pe.wait_ge(lo_made, i * RING + (T_VV + 2 * g + 2))
                pe.wait_ge(p_lo_made, i * RING + (2 * g + 2))
                for d in range(KT):
                    pe.wait_ge(y_used, i * 2 * KT + (KT * g + d + KT - 3))
                    out = pair[d % 4]
                    for c in range(2):
                        r = (2 * g + c) % RING
                        for w, xs in ((w_hi, (P_hi, P_lo)), (w_lo, (P_hi,))):
                            for x_part in xs:
                                for a in range(2):
                                    mm = nc.tensor.matmul(out[:, 512 * a:512 * a + HALF], w[r][:, d, :],
                                                          x_part[r][:, a, :],
                                                          start=(c == 0 and w is w_hi and x_part is P_hi),
                                                          stop=(c == 1 and w is w_lo))
                    mm.then_inc(down_done, 1)

            pe.wait_ge(out_used, T_VV + 2)
            pe.wait_ge(g_used, NTOK // UNIT + 4)
            with pe.Fori(0, DGROUPS // 2) as i:
                for g in range(2):
                    down(i, g)
            pe.wait_ge(y_used, KT * (DGROUPS + 1))
            sum_squares(2 * KT, pair[0], lambda k: sq_final[:, k, :, :])

        @block.scalar
        def _(act):
            links = [0]

            def link(ins):
                links[0] += 1
                ins.then_inc(act_chain, 1)
                act.wait_ge(act_chain, links[0])

            def weights_hi(i, t):
                r = t % RING
                act.wait_ge(raw_in[r], i * 16 + 16 * (t // RING + 1))
                if t >= RING or not isinstance(i, int):
                    act.wait_ge(tile_done, i * RING + (t - RING + 1))
                nc.scalar.activation(w_hi[r][:, :, :], w_raw[r][:, :, :], ACT.Copy).then_inc(hi_made, 1)

            def tile_phase(t0, n, step):
                with act.Fori(0, n // RING) as i:
                    for r in range(RING):
                        weights_hi(i, t0 + r + AHEAD)
                        step(i, t0, r)

            def wait_tile(i, t):
                act.wait_ge(tile_done, i * RING + (t + 1))
                act.wait_ge(out_used, i * RING + (t + 2))

            def squares(src, base, ready, out=None):
                for k in range(KT):
                    act.wait_ge(*ready(k))
                    if out is None and k >= 2:
                        act.wait_ge(sq_used, k - 1)
                    nc.scalar.activation(sq[k % 2][:, :, :] if out is None else out[:, k, :, :], src[:, k, :, :],
                                         ACT.Square).then_inc(sq_made, 1)

            def std(base, p):
                act.wait_ge(sq_used, base + KT)
                act.wait_ge(masks_made, 2)
                nc.scalar.activation(rs[:, :, :], pv[p], ACT.Sqrt, bias=eps_col[:, 0:1],
                                     scale=1.0 / D).then_inc(std_made, 1)

            def high_parts(base):
                for k in range(KT):
                    act.wait_ge(ht_made, base + k + 1)
                    nc.scalar.activation(H_hi[:, k, :, :], ht[k % 2][:, :, :], ACT.Copy).then_inc(hh_made, 1)

            squares(X, 0, lambda k: (x_in[k], 16))
            std(0, 0)
            act.wait_ge(wg_in, 16)
            nc.scalar.activation(wg_hi[:, :, :], wg_raw[:, :, :], ACT.Copy).then_inc(wg_hi_made, 1)
            high_parts(0)
            for t in range(AHEAD):
                weights_hi(0, t)
            act.wait_ge(gate_neg, 1)
            nc.scalar.activation(grow[3][32:32 + H, :], grow[4][32:32 + H, :], ACT.Exp).then_inc(gate_act, 1)
            act.wait_ge(gate_act, 1)
            nc.scalar.activation(grow[5][32:32 + H, :], grow[3][32:32 + H, :], ACT.Ln, bias=1.0).then_inc(gate_act, 1)
            act.wait_ge(row_args, 3)
            nc.scalar.activation(E_row[:, :], grow[8][0:H, :], ACT.Exp, scale=-1.0).then_inc(gate_act, 1)
            nc.scalar.activation(grow[1][0:H, :], grow[7][0:H, :], ACT.Exp).then_inc(gate_act, 1)
            nc.scalar.activation(al_row[:, :], grow[9][0:H, 0:NSAM], ACT.Exp).then_inc(gate_act, 1)

            for t in range(AHEAD, AHEAD + RING):
                weights_hi(0, t)
            with act.Fori(1, 3 * KT // RING) as i:
                for r in range(RING):
                    weights_hi(i, AHEAD + r)
            act.wait_ge(sam_zero, 1)
            for n in range(2 * NB):
                b, q = divmod(n, 2)
                rows = P if b < SB else NSAM
                act.wait_ge(tr_done, 2 * n + 1)
                dst = K_tok[:, b, :] if b < SB else k_sam[0:NSAM, :]
                nc.scalar.activation(dst[:, q * 512:(q + 1) * 512], bank(4 + (2 * n) % 4)[0:rows, :],
                                     ACT.Copy).then_inc(tr_k_used, 1)

            def decays(h):
                w_off = 0
                for s in range(SB):
                    n = SEQ - s * P
                    act.wait_ge(w_arg, SB * h + s + 1)
                    nc.scalar.activation(W[h % 2][:, w_off:w_off + n], W[h % 2][:, w_off:w_off + n], ACT.Exp,
                                         scale=-1.0).then_inc(w_exp, 1)
                    w_off += n

            decays(0)
            for h in range(H):
                act.wait_ge(num_done, h + 1)
                if h:
                    act.wait_ge(hout_made, 2 * h)
                nc.scalar.activation(r_buf[:, :], bank(7), ACT.Abs).then_inc(abs_made, 1)
                for v in range(HT):
                    act.wait_ge(hout_made, HT * h + v + 1)
                    if h:
                        act.wait_ge(head_done, h)
                        act.wait_ge(hsq_used, HT * h)
                    nc.scalar.activation(hsq[v][:, :], flat(HN)[:, h * HT + v, 0:SEQ], ACT.Square).then_inc(hsq_made, 1)
                if h + 1 < H:
                    decays(h + 1)
                act.wait_ge(st_done, h + 1)
                if h:
                    act.wait_ge(cout_stored, 16 * h)
                nc.scalar.activation(C_out[:, :, :], bank(4).rearrange("p (k v) -> p k v", k=HT),
                                     ACT.Copy).then_inc(cout_made, 1)
                act.wait_ge(cout_made, h + 1)
                act.dma_start(outs["o_cp"][h], C_out[:, :, :]).then_inc(cout_stored, 16)
                act.wait_ge(hsq_used, HT * (h + 1))
                nc.scalar.activation(hsq[0][:, :], bank(7), ACT.Sqrt, bias=eps_col[:, 0:1],
                                     scale=1.0 / DH).then_inc(hstd_made, 1)

            act.wait_ge(cout_stored, 16 * H)
            act.wait_ge(sb_done, 1)
            nc.scalar.activation(alpha_s[:, :, :], bank(1)[:, 0:P].rearrange("p (h t) -> p h t", h=H),
                                 ACT.Copy).then_inc(sam_al, 1)
            act.wait_ge(sam_arg, 1)
            nc.scalar.activation(Ws[:, :, :], Ws[:, :, :], ACT.Exp, scale=-1.0).then_inc(sam_exp, 1)

            def step_sigmoid(i, t0, r):
                wait_tile(i, t0 + r)
                nc.scalar.activation(SG[:, i * RING + r, :, :], pv[r % 2], ACT.Sigmoid).then_inc(out_used, 1)

            tile_phase(T_GB, 2 * KT, step_sigmoid)
            act.wait_ge(sam_num, H * NSEQ)
            nc.scalar.activation(rsam[:, :, :], bank(4)[:, 0:P].rearrange("p (h t) -> p h t", h=H),
                                 ACT.Abs).then_inc(sam_abs, 1)
            act.wait_ge(sam_hout, 1)
            nc.scalar.activation(sqs[:, :, :], flat(HN)[:, :, SEQ:NTOK], ACT.Square).then_inc(sam_sq, 1)
            act.wait_ge(sam_rms, 1)
            nc.scalar.activation(rss[:, :, :], bank(4)[:, 3 * P:4 * P].rearrange("p (h t) -> p h t", h=H), ACT.Sqrt,
                                 bias=eps_col[:, 0:1], scale=1.0 / DH).then_inc(sam_std, 1)

            act.wait_ge(sam_hn, 1)
            with act.Fori(0, 2) as i:
                for m in range(4):
                    for q in range(3):
                        t = 3 * m + q
                        weights_hi(3 * i, T_CONV + t + AHEAD)
                        if q == 0:
                            wait_tile(3 * i, T_CONV + t)
                            act.wait_ge(cc_used, i * 4 + (m + 1))
                            nc.scalar.activation(cc_t[:, :, :], pv[t % 2], ACT.Copy).then_inc(out_used, 1)
                        if q == 2:
                            act.wait_ge(t_made, i * 4 + (m + 1))
                            nc.scalar.activation(S_hi[:, i * 4 + m, :, :], tmp[m % 2][:, :, :],
                                                 ACT.Copy).then_inc(t_hi, 1)
            tile_phase(T_WB, KT, lambda i, t0, r: None)

            act.wait_ge(t_lo, KT)

            def step_o(i, t0, r):
                wait_tile(i, t0 + r)
                nc.scalar.activation(so_t[r % 2][:, :, :], pv[r % 2], ACT.Sigmoid).then_inc(out_used, 1)
                act.wait_ge(t_made, i * RING + (KT + r + 1))
                nc.scalar.activation(S_hi[:, i * RING + r, :, :], tmp[r % 2][:, :, :], ACT.Copy).then_inc(t_hi, 1)

            tile_phase(T_O, KT, step_o)

            def step_merge(i, t0, r):
                act.wait_ge(t_made, i * RING + (2 * KT + r + 1))
                nc.scalar.activation(M_hi[:, i * RING + r, :, :], tmp[r % 2][:, :, :], ACT.Copy).then_inc(t_hi, 1)

            tile_phase(T_WA, KT, step_merge)

            def step_square(i, t0, r):
                act.wait_ge(out_used, i * RING + (t0 + r + 3))
                nc.scalar.activation(sq_ffn[:, i * RING + r, :, :], X2[:, i * RING + r, :, :],
                                     ACT.Square).then_inc(sq_made, 1)

            tile_phase(T_WO, KT, step_square)
            std(KT, 2)
            high_parts(KT)

            def step_query(i, t0, r):
                wait_tile(i, t0 + r)
                act.wait_ge(sc_done, i * RING + (r + 1))
                nc.scalar.activation(qT[r % 2][:, :, :], pv[r % 2], ACT.Copy).then_inc(out_used, 1)

            tile_phase(T_WQ, 2 * RH, step_query)

            def expert_act(i, t, c, s):
                weights_hi(i, t + AHEAD)
                wait_tile(i, t)
                if not isinstance(i, int) or t >= T_U + 4 or i > 0:
                    act.wait_ge(a_stored[s], i * 16 + 16 * ((t - T_U) // 4))
                nc.scalar.activation(A_ring[s][:, :, :], pv[t % 2], ACT.Gelu).then_inc(out_used, 1)
                act.wait_ge(out_used, i * RING + (t + 3))
                act.dma_start(A_dram[c], A_ring[s][:, :, :].rearrange("p a b -> p (a b)")).then_inc(a_stored[s], 16)

            def route_block(b, n):
                if not isinstance(b, int) or b > 0:
                    act.wait_ge(blk_used, b)
                nc.scalar.activation(S_blk[0:n, :, :], S_all[0:n, b, :, :], ACT.Copy).then_inc(blk_made, 1)
                for r in range(ROUTE_TILES):
                    if r == ROUTE_TILES - 2:
                        act.wait_ge(sm_arg, b + 1)
                        nc.scalar.activation(small["gate"][0:n, :, :], small["gate"][0:n, :, :],
                                             ACT.Exp).then_inc(sm_exp, 1)
                    expert_act(b * (ROUTE_TILES // RING), T_U + r, b * ROUTE_TILES + r, r % 4)

            act.wait_ge(sc_used, 2 * RH + 2)
            route_block(0, P)
            with act.Fori(1, SB) as b:
                route_block(b, P)
            route_block(SB, NSAM)

            def keep_unit(i, per, u, st, col):
                act.wait_ge(g_done, i * per + (u + 3))
                nc.scalar.activation(st[:, :, col:col + UNIT],
                                     bank(4 + u % 4).rearrange("p (q k) -> p k q", q=UNIT),
                                     ACT.Copy).then_inc(g_used, 1)

            act.sem_inc(g_used, 4)
            t0 = T_U + NB * ROUTE_TILES
            upg = TILES_PER_GROUP * UNITS_PER_TILE

            TPG = TILES_PER_GROUP

            def gate_group(i, n, wait_stored):
                if wait_stored:
                    act.wait_ge(g_stored[n], i * 16)
                for r in range(TPG):
                    t = t0 + n * TPG + r
                    expert_act(i * (2 * TPG // RING), t, i * (2 * TPG) + (t - T_U), (t - T_U) % 4)
                    for u in range(UNITS_PER_TILE):
                        keep_unit(i, 2 * upg, n * upg + UNITS_PER_TILE * r + u, G_st[n],
                                  UNIT * (UNITS_PER_TILE * r + u))
                act.wait_ge(g_used, i * (2 * upg) + ((n + 1) * upg + 4))
                act.dma_start(G_dram[:, :, bass.ds(i * (2 * GTOK) + n * GTOK, GTOK)].rearrange("c p t -> p c t"),
                              G_st[n][:, :, :]).then_inc(g_stored[n], 16)

            for n in range(2):
                gate_group(0, n, False)
            with act.Fori(1, GROUPS // 2) as i:
                for n in range(2):
                    gate_group(i, n, True)
            act.wait_ge(g_stored[0], 16 * (GROUPS // 2))
            t0 += GROUPS * TPG
            for r in range(LAST_TILES):
                t = t0 + r
                expert_act(0, t, t - T_U, (t - T_U) % 4)
                for u in range(UNITS_PER_TILE):
                    keep_unit(0, 0, GROUPS * upg + UNITS_PER_TILE * r + u, G_st[0], UNIT * (UNITS_PER_TILE * r + u))
            act.wait_ge(g_used, GROUPS * upg + LAST_TILES * UNITS_PER_TILE + 4)
            act.dma_start(G_dram[:, :, SEQ:NTOK].rearrange("c p t -> p c t"),
                          G_st[0][:, :, 0:NSAM]).then_inc(g_stored[0], 16)

            weights_hi(0, T_VV + AHEAD)

            for c in range(2):
                act.wait_ge(p_made, c + 1)
                nc.scalar.activation(P_hi[c][:, :, :], PA[c][:, :, :], ACT.Copy).then_inc(p_hi_made, 1)

            def down_group(i, g, weights):
                for c in (2 * g + 2, 2 * g + 3):
                    if not isinstance(i, int) or g > 0:
                        act.wait_ge(down_done, i * 2 * KT + KT * g)
                    act.wait_ge(p_made, i * RING + (c + 1))
                    nc.scalar.activation(P_hi[c % 4][:, :, :], PA[c % 4][:, :, :], ACT.Copy).then_inc(p_hi_made, 1)
                if weights:
                    for c in (2 * g, 2 * g + 1):
                        act.wait_ge(raw_in[c % 4], i * 16 + 16 * ((T_VV + RING + c) // RING + 1))
                        act.wait_ge(down_done, i * 2 * KT + KT * (g + 1))
                        nc.scalar.activation(w_hi[c % 4][:, :, :], w_raw[c % 4][:, :, :], ACT.Copy).then_inc(hi_made, 1)

            for g in range(2):
                down_group(0, g, True)
            with act.Fori(1, DGROUPS // 2 - 1) as i:
                for g in range(2):
                    down_group(i, g, True)
            down_group(0, DGROUPS - 2, False)
            squares(X2, 2 * KT, lambda k: (y_used, KT * DGROUPS + k + 1), sq_final)
            std(2 * KT, 0)

        @block.vector
        def _(dve):
            links = [0]

            def link(ins):
                links[0] += 1
                ins.then_inc(dve_chain, 1)
                dve.wait_ge(dve_chain, links[0])

            def normalise(src, gain, base, split):
                dve.wait_ge(std_made, base // KT + 1)
                nc.vector.reciprocal(rs[:, :, :], rs[:, :, :]).then_inc(out_used if base == 0 else dve_chain, 1)
                if base == 0:
                    dve.wait_ge(out_used, 1)
                else:
                    links[0] += 1
                    dve.wait_ge(dve_chain, links[0])

                def low(k):
                    dve.wait_ge(hh_made, base + k + 1)
                    nc.vector.tensor_tensor(H_lo[:, k, :, :], ht[k % 2][:, :, :], H_hi[:, k, :, :].bitcast(F32),
                                            ALU.subtract).then_inc(hl_made, 1)

                for k in range(KT):
                    if split and k >= 2:
                        dve.wait_ge(hl_made, base + k - 1)
                    nc.vector.scalar_tensor_tensor(out=ht[k % 2][:, :, :] if split else src[:, k, :, :], in0=src[:, k, :, :],
                                                   scalar=vec[:, gain, k:k + 1], in1=rs[:, :, :], op0=ALU.mult,
                                                   op1=ALU.mult).then_inc(ht_made if split else y_made, 1)
                    if split and k:
                        low(k - 1)
                if split:
                    low(KT - 1)

            link(nc.vector.memset(v_sam[:, :], 0.0))
            nc.vector.memset(k_sam[:, :], 0.0).then_inc(sam_zero, 1)
            dve.wait_ge(consts_in, 16 * 5)
            dve.wait_ge(wg_hi_made, 1)
            nc.vector.tensor_tensor(wg_lo[:, :, :], wg_raw[:, :, :], wg_hi[:, :, :].bitcast(F32),
                                    ALU.subtract).then_inc(wg_lo_made, 1)
            for k in range(KT):
                dve.wait_ge(x_in[k], 16)
            normalise(X, G_MIX, 0, True)

            dve.wait_ge(gate_done, 1)
            F = slice(32, 32 + H)
            HS = slice(0, H)
            gv = [g[:, :].rearrange("p (a b) -> p a b", a=2) for g in grow]
            link(nc.vector.tensor_scalar(gv[2][F], pv[1][F], bias_if[F, :], None, ALU.add))
            nc.vector.scalar_tensor_tensor(out=gv[4][F], in0=gv[2][F], scalar=-1.0, in1=gv[2][F], op0=ALU.mult,
                                           op1=ALU.min).then_inc(gate_neg, 1)
            link(nc.vector.tensor_scalar(gv[6][HS], pv[1][HS], bias_if[HS, :], None, ALU.add))
            link(nc.vector.tensor_scalar(grow[2][F, :], grow[2][F, :], 0.0, None, ALU.min))
            dve.sem_inc(out_used, 1)
            dve.sem_inc(sc_used, 2)
            dve.sem_inc(cc_used, 1)
            dve.sem_inc(y_used, KT)
            dve.sem_inc(cn_made, 2)
            for n in range(STR):
                dve.sem_inc(cn_stored[n], 16)
            dve.wait_ge(gate_act, 2)
            logf, bcum, ones_row = grow[10], grow[11], grow[9]
            link(nc.vector.tensor_tensor(logf[HS, :], grow[2][F, :], grow[5][F, :], ALU.subtract))
            link(nc.vector.memset(ones_row[HS, :], 1.0))
            link(nc.vector.tensor_tensor_scan(bcum[HS, 0:SEQ], ones_row[HS, 0:SEQ], logf[HS, 0:SEQ], 0.0,
                                              ALU.mult, ALU.add))

            def sam(t, j):
                return t[HS, SEQ:NTOK].rearrange("p (b j) -> p b j", j=DSEQ)[:, :, j]

            link(nc.vector.tensor_copy(sam(bcum, 0), sam(logf, 0)))
            for j in range(1, DSEQ):
                link(nc.vector.tensor_tensor(sam(bcum, j), sam(bcum, j - 1), sam(logf, j), ALU.add))
            a_row = grow[0]
            link(nc.vector.tensor_tensor(a_row[HS, :], grow[6][HS, :], bcum[HS, :], ALU.subtract))
            link(nc.vector.tensor_tensor_scan(M_row[:, 0:SEQ], a_row[HS, 0:SEQ], a_row[HS, 0:SEQ], 0.0,
                                              ALU.max, ALU.max))
            link(nc.vector.tensor_tensor(sam(M_row, 0), m0_sb[:, :], sam(a_row, 0), ALU.max))
            for j in range(1, DSEQ):
                link(nc.vector.tensor_tensor(sam(M_row, j), sam(M_row, j - 1), sam(a_row, j), ALU.max))
            link(nc.vector.tensor_tensor(grow[8][HS, :], bcum[HS, :], M_row[:, :], ALU.add))
            nc.vector.tensor_copy(mp_sb[:, :], grow[8][HS, SEQ - 1:SEQ])
            nc.vector.tensor_copy(ms_sb[:, :], sam(grow[8], DSEQ - 1)).then_inc(row_args, 1)
            nc.vector.tensor_scalar(grow[7][HS, 0:SEQ], a_row[HS, 0:SEQ], M_row[:, SEQ - 1:SEQ], None, ALU.subtract)
            seqs = lambda t: t[HS, SEQ:NTOK].rearrange("p (b j) -> p b j", j=DSEQ)
            nc.vector.tensor_tensor(seqs(grow[7]), seqs(a_row),
                                    sam(M_row, DSEQ - 1).unsqueeze(2).broadcast_to([H, NSEQ, DSEQ]),
                                    ALU.subtract).then_inc(row_args, 1)
            nc.vector.tensor_tensor(grow[9][HS, 0:NSAM].rearrange("p (b j) -> p b j", j=DSEQ),
                                    m0_sb[:, :].unsqueeze(2).broadcast_to([H, NSEQ, DSEQ]), seqs(M_row),
                                    ALU.subtract).then_inc(row_args, 1)
            dve.wait_ge(gate_act, 5)
            dve.sem_inc(rows_made, 1)

            def tile_phase(t0, n, step):
                with dve.Fori(0, n // RING) as i:
                    for r in range(RING):
                        dve.wait_ge(tile_done, i * RING + (t0 + r + 1))
                        step(i, r)

            tile_phase(T_Q, KT, lambda i, r: nc.vector.tensor_copy(
                Q[:, i * RING + r, :, :], pv[r % 2]).then_inc(out_used, 1))
            tile_phase(T_K, KT, lambda i, r: nc.vector.tensor_scalar(
                K[:, i * RING + r, :, :], pv[r % 2], float(DH) ** -0.5, None, ALU.mult).then_inc(out_used, 1))
            dve.wait_ge(cols_done, 1)
            for n, (lo_b, hi_b) in ((P, (0, SB)), (NSAM, (SB, NB))):
                cols = bank(4)[0:n, 0:NB * 2 * H].rearrange("p (b j h) -> p b j h", j=2, h=H)
                nc.vector.tensor_copy(a_col[0:n, lo_b:hi_b, :], cols[:, lo_b:hi_b, 0, :])
                ins = nc.vector.tensor_copy(dec_col[0:n, lo_b:hi_b, :], cols[:, lo_b:hi_b, 1, :])
            ins.then_inc(cols_used, 1)
            tile_phase(T_V, KT, lambda i, r: nc.vector.tensor_copy(
                VT[:, i * RING + r, :, :], pv[r % 2]).then_inc(out_used, 1))
            for n in range(2 * NB):
                b, q = divmod(n, 2)
                rows = P if b < SB else NSAM
                dve.wait_ge(tr_done, 2 * n + 2)
                dst = V_tok[:, b, :] if b < SB else v_sam[0:NSAM, :]
                nc.vector.tensor_copy(dst[:, q * 512:(q + 1) * 512],
                                      bank(4 + (2 * n + 1) % 4)[0:rows, :]).then_inc(tr_v_used, 1)

            dve.wait_ge(cols_used, 1)

            def head_weights(h):
                dve.wait_ge(m_done, h + 1)
                if h >= 2:
                    dve.wait_ge(num_done, h - 1)
                w_off = []
                c = 0
                for s in range(SB):
                    w_off.append(c)
                    n = SEQ - s * P
                    nc.vector.tensor_scalar(W[h % 2][:, c:c + n], bank(3)[:, s * P:SEQ], a_col[:, s, h:h + 1], 0.0,
                                            ALU.subtract, ALU.max).then_inc(w_arg, 1)
                    c += n
                dve.wait_ge(w_exp, SB * (h + 1))
                for s in range(SB):
                    d = W[h % 2][:, w_off[s]:w_off[s] + P]
                    ins = nc.vector.tensor_tensor(d, d, causal[:, :], ALU.mult)
                link(ins)
                dve.wait_ge(s_done, h + 1)
                for s, off in enumerate((0, 512, 1024, 896)):
                    n = SEQ - s * P
                    w = W[h % 2][:, w_off[s]:w_off[s] + n]
                    ins = nc.vector.tensor_tensor(w, bank(off // 512)[:, off % 512:off % 512 + n], w, ALU.mult)
                ins.then_inc(sw_made, 1)

            head_weights(0)
            for h in range(H):
                if h:
                    dve.wait_ge(st_done, h)
                nc.vector.tensor_tensor(dV[:, :, :], V_tok[:, 0:SB, h * DH:(h + 1) * DH],
                                        dec_col[:, 0:SB, h:h + 1].broadcast_to([P, SB, DH]), ALU.mult).then_inc(dv_made, 1)
                dve.wait_ge(abs_made, h + 1)
                nc.vector.tensor_tensor(r_buf[:, :], r_buf[:, :], bank(3), ALU.max).then_inc(e_used, 1)
                dve.wait_ge(e_used, h + 1)
                link(nc.vector.reciprocal(r_buf[:, :], r_buf[:, :]))
                for v in range(HT):
                    nc.vector.tensor_tensor(flat(HN)[:, h * HT + v, 0:SEQ], bank(5 + v), r_buf[:, :],
                                            ALU.mult).then_inc(hout_made, 1)
                dve.wait_ge(n_done, h + 1)
                nc.vector.tensor_copy(np_sb[:, h * HT:(h + 1) * HT], bank(7)[:, 0:HT]).then_inc(n_used, 1)
                if h + 1 < H:
                    head_weights(h + 1)
                dve.wait_ge(hstd_made, h + 1)
                link(nc.vector.reciprocal(hsq[0][:, :], hsq[0][:, :]))
                for v in range(HT):
                    hn = flat(HN)[:, h * HT + v, 0:SEQ]
                    ins = nc.vector.scalar_tensor_tensor(out=hn, in0=hn, scalar=vec[:, G_HEAD, h * HT + v:h * HT + v + 1],
                                                         in1=hsq[0][:, :], op0=ALU.mult, op1=ALU.mult)
                ins.then_inc(head_done, 1)

            def heads(ap):
                return ap.rearrange("p (h t) -> p h t", h=H)

            dve.wait_ge(sb_done, 1)
            link(nc.vector.memset(dm[:, :, :], 0.0))
            nc.vector.tensor_tensor(dm[0:NSAM, :, :], dec_col[0:NSAM, SB, :].unsqueeze(2).broadcast_to([NSAM, H, NSEQ]),
                                    seq_mask[:, :].unsqueeze(1).broadcast_to([NSAM, H, NSEQ]), ALU.mult)
            link(nc.vector.tensor_tensor(Ws[:, :, :], heads(bank(0)[0:NSAM, P:2 * P]),
                                         a_col[0:NSAM, SB, :].unsqueeze(2).broadcast_to([NSAM, H, NSAM]), ALU.subtract))
            nc.vector.tensor_scalar(Ws[:, :, :], Ws[:, :, :], 0.0, None, ALU.max).then_inc(sam_arg, 1)
            dve.wait_ge(sam_al, 1)
            link(nc.vector.tensor_tensor(
                q_al[:, :, :].rearrange("p (h k) t -> p h k t", k=HT),
                flat(Q)[:, :, SEQ:NTOK].rearrange("p (h k) t -> p h k t", k=HT),
                alpha_s[:, :, :].unsqueeze(2).broadcast_to([P, H, HT, NSAM]), ALU.mult))
            nc.vector.tensor_tensor(qn[:, :, :].rearrange("p f (b j) -> p f b j", j=DSEQ),
                                    q_al[:, :, :].rearrange("p f (b j) -> p f b j", j=DSEQ),
                                    n0_sb[:, :, :].unsqueeze(3).broadcast_to([P, H * HT, NSEQ, DSEQ]), ALU.mult)
            dve.wait_ge(sam_exp, 1)
            link(nc.vector.tensor_tensor(Ws[:, :, :], Ws[:, :, :], sam_mask[:, :, :].rearrange("p b j -> p (b j)")
                                         .unsqueeze(1).broadcast_to([NSAM, H, NSAM]), ALU.mult))
            nc.vector.tensor_tensor(Ws[:, :, :], heads(bank(0)[0:NSAM, 0:P]), Ws[:, :, :], ALU.mult).then_inc(sam_sw, 1)
            with dve.Fori(0, H) as i:
                for u in range(NSEQ):
                    dve.wait_ge(upd_done, i * NSEQ + (u + 1))
                    nc.vector.tensor_scalar(km[u % 2][:, :], k_sam[:, bass.ds(i * DH, DH)],
                                            dm[:, :, :].rearrange("p h b -> p (h b)")[:, bass.ds(i * NSEQ + u, 1)],
                                            None, ALU.mult).then_inc(km_made, 1)
                    dve.wait_ge(upd_done, i * NSEQ + (u + 3))
                    dve.wait_ge(c0_in[u % STR], i * (16 * (NSEQ // STR)) + 16 * (u // STR + 1))
                    dve.wait_ge(cn_stored[u % STR], i * (16 * (NSEQ // STR)) + 16 * (u // STR + 1))
                    nc.vector.scalar_tensor_tensor(
                        out=cn_ring[u % STR][:, :, :].rearrange("p k v -> p (k v)"),
                        in0=c0_ring[u % STR][:, :, :].rearrange("p k v -> p (k v)"),
                        scalar=alpha_s[:, :, :].rearrange("p h t -> p (h t)")
                        [:, bass.ds(i * NSAM + (u * DSEQ + DSEQ - 1), 1)],
                        in1=bank(6 + u % 2), op0=ALU.mult, op1=ALU.add).then_inc(cn_made, 1)
            a_end = alpha_s[:, :, :].rearrange("p h (b j) -> p h b j", j=DSEQ)[:, :, :, DSEQ - 1]
            link(nc.vector.tensor_tensor(ns_sb[:, :, :].rearrange("p (h k) b -> p h k b", k=HT),
                                         n0_sb[:, :, :].rearrange("p (h k) b -> p h k b", k=HT),
                                         a_end.unsqueeze(2).broadcast_to([P, H, HT, NSEQ]), ALU.mult))
            dve.wait_ge(sam_abs, 1)
            nc.vector.tensor_tensor(ns_sb[:, :, :], bank(4)[:, P:P + H * HT * NSEQ].rearrange("p (f b) -> p f b", b=NSEQ),
                                    ns_sb[:, :, :], ALU.add)
            link(nc.vector.tensor_tensor(rsam[:, :, :], rsam[:, :, :], heads(bank(4)[:, 2 * P:3 * P]), ALU.max))
            link(nc.vector.reciprocal(rsam[:, :, :], rsam[:, :, :]))
            hs = flat(HN)[:, :, SEQ:NTOK]
            hs4 = hs.rearrange("p (h k) t -> p h k t", k=HT)
            nc.vector.tensor_tensor(hs4, bank(5)[:, 0:2 * P].rearrange("p (h k t) -> p h k t", h=H, k=HT),
                                    rsam[:, :, :].unsqueeze(2).broadcast_to([P, H, HT, NSAM]),
                                    ALU.mult).then_inc(sam_hout, 1)
            dve.wait_ge(sam_std, 1)
            link(nc.vector.reciprocal(rss[:, :, :], rss[:, :, :]))
            dve.wait_ge(sam_hout, 1)
            link(nc.vector.tensor_tensor(hs4, hs4, rss[:, :, :].unsqueeze(2).broadcast_to([P, H, HT, NSAM]), ALU.mult))
            link(nc.vector.tensor_tensor(hs, hs, vec[:, G_HEAD, :].unsqueeze(2).broadcast_to([P, KT, NSAM]), ALU.mult))
            dve.wait_ge(head_done, H)
            for n in range(STR):
                dve.wait_ge(cn_stored[n], 16 + 16 * (H * NSEQ // STR))
            dve.sem_inc(sam_hn, 1)

            def low(i, j, n, lo, hi, dst, count):
                dve.wait_ge(t_hi, count)
                nc.vector.tensor_tensor(lo[:, dst, :, :], tmp[n][:, :, :], hi[:, dst, :, :].bitcast(F32),
                                        ALU.subtract).then_inc(t_lo, 1)
                dve.wait_ge(t_lo, count)

            conv_steps = 9
            conv_base = links[0]
            with dve.Fori(0, 2) as i:
                for m in range(4):
                    j = i * 4 + m
                    k0 = [m * conv_steps]

                    def clink(ins):
                        k0[0] += 1
                        ins.then_inc(dve_chain, 1)
                        dve.wait_ge(dve_chain, i * (4 * conv_steps) + (conv_base + k0[0]))

                    uf = u_t[:, :, :].rearrange("p a b -> p (a b)")
                    yf = y_t[:, :, :].rearrange("p a b -> p (a b)")
                    dve.wait_ge(out_used, i * 12 + (T_CONV + 3 * m + 3))
                    dve.wait_ge(tile_done, i * 12 + (T_CONV + 3 * m + 2))
                    nc.vector.tensor_tensor(u_t[:, :, :], pv[(3 * m + 1) % 2], cc_t[:, :, :], ALU.mult).then_inc(out_used, 1)
                    dve.wait_ge(out_used, i * 12 + (T_CONV + 3 * m + 4))
                    dve.sem_inc(cc_used, 1)
                    wc = [vec[:, G_CONV + q, bass.ds(j, 1)] for q in range(3)]
                    clink(nc.vector.tensor_scalar(y_t[:, :, :], u_t[:, :, :], wc[2], None, ALU.mult))
                    for q, lag in ((1, 1), (0, 2)):
                        clink(nc.vector.scalar_tensor_tensor(out=yf[:, lag:SEQ], in0=uf[:, 0:SEQ - lag], scalar=wc[q],
                                                             in1=yf[:, lag:SEQ], op0=ALU.mult, op1=ALU.add))
                    clink(nc.vector.tensor_copy(ext[:, :, 0:2], conv0_sb[:, j, :, :]))
                    clink(nc.vector.tensor_copy(ext[:, :, 2:2 + DSEQ],
                                                uf[:, SEQ:NTOK].rearrange("p (b j) -> p b j", j=DSEQ)))
                    ys = yf[:, SEQ:NTOK].rearrange("p (b j) -> p b j", j=DSEQ)
                    for q in (1, 0):
                        clink(nc.vector.scalar_tensor_tensor(out=ys, in0=ext[:, :, q:q + DSEQ], scalar=wc[q], in1=ys,
                                                             op0=ALU.mult, op1=ALU.add))
                    clink(nc.vector.tensor_copy(convp_sb[:, j, :], uf[:, SEQ - 2:SEQ]))
                    clink(nc.vector.tensor_copy(convs_sb[:, j, :, :], ext[:, :, DSEQ:DSEQ + 2]))
                    dve.wait_ge(tile_done, i * 12 + (T_CONV + 3 * m + 3))
                    nc.vector.tensor_tensor(tmp[m % 2][:, :, :], pv[(3 * m + 2) % 2], y_t[:, :, :],
                                            ALU.mult).then_inc(t_made, 1)
                    dve.wait_ge(t_made, i * 4 + (m + 1))
                    dve.sem_inc(out_used, 1)
                    low(i, j, m % 2, S_lo, S_hi, j, i * 4 + (m + 1))
            links[0] += 8 * conv_steps

            tile_phase(T_WB, KT, lambda i, r: nc.vector.tensor_tensor(
                M1[:, i * RING + r, :, :], pv[r % 2], SG[:, i * RING + r, :, :], ALU.mult).then_inc(out_used, 1))

            def step_ha(i, r):
                j = i * RING + r
                dve.wait_ge(out_used, i * RING + (T_O + r + 3))
                nc.vector.tensor_tensor(tmp[r % 2][:, :, :], so_t[r % 2][:, :, :], HN[:, j, :, :],
                                        ALU.mult).then_inc(t_made, 1)
                low(i, j, r % 2, S_lo, S_hi, j, i * RING + (KT + r + 1))

            tile_phase(T_O, KT, step_ha)

            def step_merge(i, r):
                j = i * RING + r
                nc.vector.tensor_tensor(tmp[r % 2][:, :, :], pv[r % 2], SG[:, i * RING + (KT + r), :, :], ALU.mult).then_inc(out_used, 1)
                dve.wait_ge(out_used, i * RING + (T_WA + r + 3))
                nc.vector.tensor_tensor(tmp[r % 2][:, :, :], tmp[r % 2][:, :, :], M1[:, j, :, :],
                                        ALU.add).then_inc(t_made, 1)
                low(i, j, r % 2, M_lo, M_hi, j, i * RING + (2 * KT + r + 1))

            dve.wait_ge(out_used, T_WA + 2)
            tile_phase(T_WA, KT, step_merge)
            dve.wait_ge(xa_in, 16)
            tile_phase(T_WO, KT, lambda i, r: nc.vector.tensor_tensor(
                X2[:, i * RING + r, :, :], pv[r % 2], X_again[:, i * RING + r, :, :], ALU.add).then_inc(out_used, 1))
            normalise(X2, G_FFN, KT, True)

            with dve.Fori(0, 2 * RH // RING) as i:
                for r in range(RING):
                    dve.wait_ge(sc_done, i * RING + (r + 3))
                    j = i * RING + r
                    nc.vector.tensor_copy(S_all[:, 0:SB, j, :],
                                          pair[2 + r % 2][:, 0:SB * P].rearrange("p (b k) -> p b k", k=NKEY))
                    nc.vector.tensor_copy(S_all[0:NSAM, SB, j, :],
                                          pair[2 + r % 2][0:NSAM, SB * P:NB * P]).then_inc(sc_used, 1)

            def route(b, n):
                val, ind, indf = small["val"], small["ind"], small["indf"]
                best, pos, posw, posf = small["best"], small["pos"], small["posw"], small["posf"]
                e1, e2, gate, zsum = small["e1"], small["e2"], small["gate"], small["zsum"]

                def top16(src, vals, inds, rows):
                    for half in range(2):
                        c = slice(8 * half, 8 * half + 8)
                        for j in range(rows):
                            ins = nc.vector.max(vals[0:n, j, c], src(j))
                        link(ins)
                        for j in range(rows):
                            ins = nc.vector.max_index(inds[0:n, j, c], vals[0:n, j, c], src(j))
                        link(ins)
                        if half == 0:
                            for j in range(rows):
                                ins = nc.vector.match_replace(out=src(j), in_to_replace=vals[0:n, j, c],
                                                              in_values=src(j), imm_value=NEG)
                            link(ins)

                dve.wait_ge(blk_made, b + 1)
                top16(lambda j: S_blk[0:n, j, :], val, ind, 2 * RH)
                dve.sem_inc(blk_used, 1)
                v4 = val[0:n, :, :].rearrange("p (h s) k -> p h s k", s=2)
                full = [n, RH, TOPK, TOPK]
                nc.vector.tensor_copy(indf[0:n, :, :], ind[0:n, :, :])
                link(nc.vector.tensor_tensor(cand[0:n, :, :, :], v4[:, :, 0, :].unsqueeze(3).broadcast_to(full),
                                              v4[:, :, 1, :].unsqueeze(2).broadcast_to(full), ALU.add))
                top16(lambda h: cand[0:n, h, :, :].rearrange("p a b -> p (a b)"), best, pos, RH)
                link(nc.vector.tensor_tensor(gate[0:n, :, :], best[0:n, :, :],
                                              best[0:n, :, 0:1].broadcast_to([n, RH, TOPK]), ALU.subtract))
                dve.sem_inc(sm_arg, 1)
                i4 = indf[0:n, :, :].rearrange("p (h s) k -> p h s k", s=2)
                for s, out in ((0, e1), (1, e2)):
                    if s == 0:
                        link(nc.vector.tensor_scalar(posw[0:n, :, :], pos[0:n, :, :], 4, None, ALU.logical_shift_right))
                    else:
                        link(nc.vector.tensor_scalar(posw[0:n, :, :], pos[0:n, :, :], TOPK - 1, None, ALU.bitwise_and))
                    link(nc.vector.tensor_copy(posf[0:n, :, :], posw[0:n, :, :]))
                    link(nc.vector.tensor_tensor(eq[0:n, :, :, :], posf[0:n, :, :].unsqueeze(3).broadcast_to(full),
                                                  iota16[0:n, :].unsqueeze(1).unsqueeze(1).broadcast_to(full),
                                                  ALU.is_equal))
                    link(nc.vector.tensor_tensor(pr[0:n, :, :, :], eq[0:n, :, :, :],
                                                  i4[:, :, s, :].unsqueeze(2).broadcast_to(full), ALU.mult))
                    link(nc.vector.tensor_reduce(out[0:n, :, :], pr[0:n, :, :, :], AX_X, ALU.add))
                dve.wait_ge(sm_exp, b + 1)
                link(nc.vector.tensor_reduce(zsum[0:n, :], gate[0:n, :, :], AX_X, ALU.add))
                link(nc.vector.reciprocal(zsum[0:n, :], zsum[0:n, :]))
                link(nc.vector.tensor_tensor(gate[0:n, :, :], gate[0:n, :, :],
                                              zsum[0:n, :].unsqueeze(2).broadcast_to([n, RH, TOPK]), ALU.mult))
                dve.sem_inc(choice_made, 1)
                dve.wait_ge(ct_done, b + 1)
                t = slice(0, n)
                cols = bass.ds(b * P, n)
                nc.vector.tensor_copy(i1T[:, cols], bank(4)[:, 0:n])
                nc.vector.tensor_copy(i2T[:, cols], bank(4)[:, P:P + n])
                nc.vector.tensor_copy(gT[:, cols], bank(4)[:, 2 * P:2 * P + n]).then_inc(ct_used, 1)

            for b in range(NB):
                route(b, P if b < SB else NSAM)

            dve.wait_ge(ct_used, NB)
            PER = 4
            base = links[0]
            block4 = [P, UNIT, NKEY]
            with dve.Fori(0, NTOK // UNIT // PER) as i:
                for u in range(PER):
                    t = bass.ds(i * (PER * UNIT) + u * UNIT, UNIT)
                    dve.wait_ge(g_done, i * PER + (u + 1))
                    nc.vector.tensor_tensor(A1[u % 2][:, :, :], iota[:, :].unsqueeze(1).broadcast_to(block4),
                                            i1T[:, t].unsqueeze(2).broadcast_to(block4),
                                            ALU.is_equal).then_inc(dve_chain, 1)
                    nc.vector.tensor_tensor(O2[u % 2][:, :, :], iota[:, :].unsqueeze(1).broadcast_to(block4),
                                            i2T[:, t].unsqueeze(2).broadcast_to(block4), ALU.is_equal)
                    dve.wait_ge(dve_chain, i * PER + (base + u + 1))
                    nc.vector.tensor_tensor(A1[u % 2][:, :, :], A1[u % 2][:, :, :],
                                            gT[:, t].unsqueeze(2).broadcast_to(block4), ALU.mult).then_inc(onehot_made, 1)
            links[0] += NTOK // UNIT

            def gated(i, c):
                s = c % 4
                dve.wait_ge(ag_in[s], i * 32 + 32 * (c // 4 + 1))
                nc.vector.tensor_tensor(PA[s][:, :, :], PA[s][:, :, :], PG[s][:, :, :], ALU.mult).then_inc(p_made, 1)

            def gated_lo(i, c):
                s = c % 4
                dve.wait_ge(p_hi_made, i * RING + (c + 1))
                nc.vector.tensor_tensor(P_lo[s][:, :, :], PA[s][:, :, :], P_hi[s][:, :, :].bitcast(F32),
                                        ALU.subtract).then_inc(p_lo_made, 1)

            def add(i, g, d):
                dve.wait_ge(down_done, i * 2 * KT + (KT * g + d + 1))
                dve.wait_ge(y_used, i * 2 * KT + (KT * g + d + 1))
                nc.vector.tensor_tensor(X2[:, d, :, :], pv[d % 4], X2[:, d, :, :], ALU.add).then_inc(y_used, 1)

            def group(i, g, more):
                if more:
                    gated(i, 2 * g + 2)
                    gated(i, 2 * g + 3)
                for d in range(KT):
                    if d == 2 and more:
                        gated_lo(i, 2 * g + 2)
                        gated_lo(i, 2 * g + 3)
                    add(i, g, d)

            for c in range(2):
                gated(0, c)
            for c in range(2):
                gated_lo(0, c)
            with dve.Fori(0, DGROUPS // 2 - 1) as i:
                for g in range(2):
                    group(i, g, True)
            group(0, DGROUPS - 2, True)
            group(0, DGROUPS - 1, False)
            normalise(X2, G_FINAL, 2 * KT, False)


def kernel(**inputs):
    import numpy as np
    import concourse.bacc as bacc
    from concourse.bass_utils import run_bass_kernel_spmd

    a = {k: np.asarray(v) for k, v in inputs.items()}

    def tiles(w):
        return w.reshape(KT, P, -1, P).transpose(2, 1, 0, 3)

    def by_feature(v):
        return v.reshape(-1, KT, P).transpose(2, 0, 1)

    w_in = a["w_in"][0]
    cols = np.cumsum([0, D, D, D, D, H, H, D, D, D, D, D])
    q, k, v, o, ig, fg, cb, cc, cx, ga, gb = (w_in[:, cols[n]:cols[n + 1]] for n in range(11))
    conv = np.stack([tiles(cc), tiles(cx), tiles(cb)], axis=1).reshape(3 * KT, P, KT, P)
    stream = np.concatenate([
        tiles(q), tiles(k), tiles(v), tiles(gb), tiles(ga), conv, tiles(a["w_out_b"][0]), tiles(o),
        tiles(a["w_out_a"][0]), tiles(a["w_o"][0]), tiles(a["w_query"][0]), tiles(a["expert_u"][0].T),
        a["expert_v"][0].reshape(CHUNKS, P, KT, P)])
    wgate = np.zeros((D, P), np.float32)
    wgate[:, 0:H] = ig
    wgate[:, 32:32 + H] = fg
    bif = np.zeros((P, 1), np.float32)
    bif[0:H, 0] = a["b_if"][0][:H]
    bif[32:32 + H, 0] = a["b_if"][0][H:]
    x = np.concatenate([a["x_prompt"].reshape(SEQ, D), a["x_sample"].reshape(NSAM, D)])
    keys = np.stack([a["sub_keys1"][0], a["sub_keys2"][0]], axis=1).reshape(2 * RH, NKEY, P)
    arrays = {
        "x": x.reshape(NTOK, KT, P).transpose(2, 1, 0),
        "wtiles": stream,
        "wgate": tiles(wgate)[0],
        "keysT": keys.transpose(2, 0, 1),
        "c0T": a["state_mlstm_C"][0].transpose(1, 0, 3, 2).reshape(H * NSEQ, HT, P, DH).transpose(0, 2, 1, 3),
        "n0T": a["state_mlstm_n"][0].reshape(NSEQ, H * HT, P).transpose(2, 1, 0),
        "m0": a["state_mlstm_m"][0].T,
        "conv0": a["state_conv"][0].reshape(NSEQ, 2, KT, P).transpose(3, 2, 0, 1),
        "vecs": np.concatenate([by_feature(a["norm_mix"]), by_feature(a["head_norm"][0]), by_feature(a["conv_w"][0]),
                                by_feature(a["norm_ffn"]), by_feature(a["norm_final"])], axis=1),
        "bif": bif,
    }
    arrays = {n: np.ascontiguousarray(t) for n, t in arrays.items()}
    nc = bacc.Bacc("TRN2", target_bir_lowering=False, num_devices=1)
    ins = [nc.dram_tensor(f"in_{n}", t.shape, mybir.dt.from_np(t.dtype), kind="ExternalInput").ap()
           for n, t in arrays.items()]
    outs = {n: nc.dram_tensor(n, s, F32, kind="ExternalOutput").ap() for n, s in OUTS.items()}
    build(nc, *ins, outs)
    r = run_bass_kernel_spmd(nc, [{f"in_{n}": t for n, t in arrays.items()}], core_ids=[0]).results[0]
    y = r["o_y"].transpose(2, 1, 0).reshape(NTOK, D)
    return (
        y[:SEQ].reshape(1, SEQ, D), y[SEQ:].reshape(NSEQ, DSEQ, D),
        r["o_cp"].transpose(0, 3, 2, 1).reshape(1, 1, H, DH, DH),
        r["o_np"].transpose(1, 0).reshape(1, 1, H, DH),
        r["o_mp"].reshape(1, 1, H),
        r["o_convp"].transpose(2, 1, 0).reshape(1, 1, 2, D),
        r["o_cs"].transpose(0, 3, 2, 1).reshape(H, NSEQ, DH, DH).transpose(1, 0, 2, 3)[None],
        r["o_ns"].transpose(2, 1, 0).reshape(1, NSEQ, H, DH),
        r["o_ms"].T[None],
        r["o_convs"].transpose(2, 3, 1, 0).reshape(1, NSEQ, 2, D),
    )
```
